# Optimizing a Trainium2 kernel written in Bass

```python
import math
import jax
import jax.numpy as jnp
from jax import lax
import numpy as np

D_MODEL = 1024
BATCH = 1
SEQ = 512
DEPTH = 2

PLE_DIM = 256
D_FF = 2816
HEAD_DIM = 64
QBLK = 128
NUM_BUCKETS = 32
MAX_DISTANCE = 128
NEG = -1e30
FORCE = 1e6
EPS = 1e-6

NSA_HEADS = 6
NSA_KV_HEADS = 2
NSA_GROUP = NSA_HEADS // NSA_KV_HEADS
CMP_BLOCK = 32
CMP_STRIDE = 16
CMP_HIDDEN = 256
SLC_BLOCK = 64
N_SELECT = 16
WINDOW = 512

DIFF_HEADS = 4
DIFF_QK_DIM = HEAD_DIM // 2

HGRN_HEADS = 6
HGRN_KEY_DIM = 64
HGRN_VAL_DIM = 64
HGRN_CHUNK = 64

NSA_WIDTH = NSA_HEADS * HEAD_DIM
KV_WIDTH = NSA_KV_HEADS * HEAD_DIM
DIFF_WIDTH = DIFF_HEADS * HEAD_DIM
HGRN_WIDTH = HGRN_HEADS * HGRN_VAL_DIM
HGRN_KEY_WIDTH = HGRN_HEADS * HGRN_KEY_DIM
MIX_WIDTH = NSA_WIDTH + DIFF_WIDTH + HGRN_WIDTH
N_BIAS_HEADS = NSA_HEADS + DIFF_HEADS

IN_SIZES = (NSA_WIDTH, KV_WIDTH, KV_WIDTH, KV_WIDTH, KV_WIDTH, KV_WIDTH, KV_WIDTH, NSA_HEADS * 3,
            DIFF_WIDTH, DIFF_WIDTH, DIFF_WIDTH,
            HGRN_KEY_WIDTH, HGRN_KEY_WIDTH, HGRN_WIDTH, HGRN_WIDTH)
IN_WIDTH = NSA_WIDTH + 6 * KV_WIDTH + 3 * NSA_HEADS + 3 * DIFF_WIDTH + 2 * HGRN_KEY_WIDTH + 2 * HGRN_WIDTH

kernel_name = 'hybrid_nsa_diff_hgrn2_macaron'

def rms_norm(x, gain):
    xf = x.astype(jnp.float32)
    xf = xf * lax.rsqrt(jnp.mean(xf * xf, axis=-1, keepdims=True) + EPS)
    return (xf * gain.astype(jnp.float32)).astype(x.dtype)

def swiglu(h, w_gate, w_up, w_down):
    return (jax.nn.silu(h @ w_gate) * (h @ w_up)) @ w_down

def t5_bucket(dist):
    n = jnp.maximum(dist, 0)
    max_exact = NUM_BUCKETS // 2
    nf = jnp.maximum(n, 1).astype(jnp.float32)
    far = max_exact + (jnp.log(nf / max_exact) / math.log(MAX_DISTANCE / max_exact)
                       * (NUM_BUCKETS - max_exact)).astype(jnp.int32)
    return jnp.where(n < max_exact, n, jnp.minimum(far, NUM_BUCKETS - 1))

def split_cols(z):
    bounds = np.cumsum(IN_SIZES)[:-1].tolist()
    return jnp.split(z, bounds, axis=-1)

def nsa_compress(kv, pos, w1, w2):
    b, t, hk, d = kv.shape
    halves = kv.reshape(b, t // CMP_STRIDE, CMP_STRIDE, hk, d)
    win = jnp.concatenate([halves[:, :-1], halves[:, 1:]], axis=2)
    win = win + pos[:, None, :]
    n = win.shape[1]
    flat = jnp.moveaxis(win, 3, 2).reshape(b, n, hk, CMP_BLOCK * d)
    return jax.nn.gelu(flat @ w1) @ w2

def nsa_attention(q, kc, vc, ks, vs, kw, vw, gates, bias_tab):
    b, t = q.shape[:2]
    n_cmp = kc.shape[1]
    n_slc = t // SLC_BLOCK
    n_sel = min(N_SELECT, n_slc)
    scale = HEAD_DIM ** -0.5
    qg = q.reshape(b, t, NSA_KV_HEADS, NSA_GROUP, HEAD_DIM)
    gg = gates.reshape(b, t, NSA_KV_HEADS, NSA_GROUP, 3)
    ks_blk = ks.reshape(b, n_slc, SLC_BLOCK, NSA_KV_HEADS, HEAD_DIM).transpose(0, 3, 1, 2, 4)
    vs_blk = vs.reshape(b, n_slc, SLC_BLOCK, NSA_KV_HEADS, HEAD_DIM).transpose(0, 3, 1, 2, 4)
    kw_pad = jnp.pad(kw, ((0, 0), (WINDOW, 0), (0, 0), (0, 0)))
    vw_pad = jnp.pad(vw, ((0, 0), (WINDOW, 0), (0, 0), (0, 0)))
    cmp_start = jnp.arange(n_cmp) * CMP_STRIDE
    slc_start = jnp.arange(n_slc) * SLC_BLOCK
    overlap = (jnp.maximum(jnp.minimum(cmp_start[:, None] + CMP_BLOCK, slc_start[None, :] + SLC_BLOCK)
                           - jnp.maximum(cmp_start[:, None], slc_start[None, :]), 0) / CMP_BLOCK).astype(jnp.float32)
    tab_sel = bias_tab.reshape(NUM_BUCKETS, NSA_KV_HEADS, NSA_GROUP).transpose(2, 1, 0).reshape(
        NSA_GROUP, NSA_KV_HEADS * NUM_BUCKETS)
    b_idx = jnp.arange(b)[:, None, None, None]
    g_idx = jnp.arange(NSA_KV_HEADS)[None, :, None, None]
    qoff = jnp.arange(QBLK)
    woff = jnp.arange(WINDOW + QBLK)
    tokoff = jnp.arange(SLC_BLOCK)

    def block(qb):
        q0 = qb * QBLK
        tpos = q0 + qoff
        qblk = lax.dynamic_slice_in_dim(qg, q0, QBLK, axis=1)
        s_c = jnp.einsum('bqgrd,bngd->bgrqn', qblk, kc).astype(jnp.float32) * scale
        valid_c = (cmp_start + CMP_BLOCK - 1)[None, :] <= tpos[:, None]
        p_c = jax.nn.softmax(jnp.where(valid_c, s_c, NEG), axis=-1) * jnp.any(valid_c, axis=-1)[:, None]
        o_c = jnp.einsum('bgrqn,bngd->bqgrd', p_c.astype(vc.dtype), vc)
        imp = jnp.einsum('bgrqn,nm->bgqm', p_c, overlap)
        blk = jnp.arange(n_slc)[None, :]
        cur = (tpos // SLC_BLOCK)[:, None]
        forced = (blk == 0) | (blk == cur) | (blk == cur - 1)
        imp = jnp.where(forced, FORCE, imp)
        imp = jnp.where(blk * SLC_BLOCK > tpos[:, None], NEG, imp)
        _, sel = lax.top_k(imp, n_sel)
        k_sel = ks_blk[b_idx, g_idx, sel].reshape(b, NSA_KV_HEADS, QBLK, n_sel * SLC_BLOCK, HEAD_DIM)
        v_sel = vs_blk[b_idx, g_idx, sel].reshape(b, NSA_KV_HEADS, QBLK, n_sel * SLC_BLOCK, HEAD_DIM)
        s_pos = (sel[..., None] * SLC_BLOCK + tokoff).reshape(b, NSA_KV_HEADS, QBLK, n_sel * SLC_BLOCK)
        dist = tpos[:, None] - s_pos
        bias = jnp.take(tab_sel, g_idx * NUM_BUCKETS + t5_bucket(dist), axis=1)
        s_s = jnp.einsum('bqgrd,bgqkd->bgrqk', qblk, k_sel).astype(jnp.float32) * scale + jnp.moveaxis(bias, 0, 2)
        p_s = jax.nn.softmax(jnp.where((dist >= 0)[:, :, None], s_s, NEG), axis=-1)
        o_s = jnp.einsum('bgrqk,bgqkd->bqgrd', p_s.astype(vs.dtype), v_sel)
        k_win = lax.dynamic_slice_in_dim(kw_pad, q0, WINDOW + QBLK, axis=1)
        v_win = lax.dynamic_slice_in_dim(vw_pad, q0, WINDOW + QBLK, axis=1)
        w_pos = q0 - WINDOW + woff
        dist_w = tpos[:, None] - w_pos[None, :]
        valid_w = (dist_w >= 0) & (dist_w < WINDOW) & (w_pos >= 0)[None, :]
        bias_w = bias_tab[t5_bucket(dist_w)].transpose(2, 0, 1).reshape(NSA_KV_HEADS, NSA_GROUP, QBLK, WINDOW + QBLK)
        s_w = jnp.einsum('bqgrd,bkgd->bgrqk', qblk, k_win).astype(jnp.float32) * scale + bias_w
        p_w = jax.nn.softmax(jnp.where(valid_w, s_w, NEG), axis=-1)
        o_w = jnp.einsum('bgrqk,bkgd->bqgrd', p_w.astype(vw.dtype), v_win)
        g = lax.dynamic_slice_in_dim(gg, q0, QBLK, axis=1)
        out = g[..., 0:1] * o_c + g[..., 1:2] * o_s + g[..., 2:3] * o_w
        return out.reshape(b, QBLK, NSA_WIDTH)

    out = lax.map(block, jnp.arange(t // QBLK))
    return jnp.moveaxis(out, 0, 1).reshape(b, t, NSA_WIDTH)

def diff_attention(q, k, v, lam, bias_tab):
    b, t = q.shape[:2]
    scale = DIFF_QK_DIM ** -0.5
    kpos = jnp.arange(t)
    qoff = jnp.arange(QBLK)

    def block(qb):
        q0 = qb * QBLK
        tpos = q0 + qoff
        qblk = lax.dynamic_slice_in_dim(q, q0, QBLK, axis=1)
        dist = tpos[:, None] - kpos[None, :]
        bias = bias_tab[t5_bucket(dist)].transpose(2, 0, 1)[None, :, None]
        s = jnp.einsum('bqhmd,bkhmd->bhmqk', qblk, k).astype(jnp.float32) * scale + bias
        p = jax.nn.softmax(jnp.where(dist >= 0, s, NEG), axis=-1)
        a = p[:, :, 0] - lam * p[:, :, 1]
        return jnp.einsum('bhqk,bkhd->bqhd', a.astype(v.dtype), v)

    out = lax.map(block, jnp.arange(t // QBLK))
    return jnp.moveaxis(out, 0, 1).reshape(b, t, DIFF_HEADS, HEAD_DIM)

def hgrn2_scan(q, k, v, log_f):
    b, t, h, dk = q.shape
    dv = v.shape[-1]
    nc = t // HGRN_CHUNK

    def chunks(a):
        return a.astype(jnp.float32).reshape(b, nc, HGRN_CHUNK, h, a.shape[-1]).transpose(1, 0, 3, 2, 4)

    causal = jnp.tril(jnp.ones((HGRN_CHUNK, HGRN_CHUNK), dtype=bool))

    def step(state, inp):
        qc, kc, vc, gc = inp
        cum = jnp.cumsum(gc, axis=2)
        inter = jnp.einsum('bhck,bhkv->bhcv', qc * jnp.exp(cum), state)
        decay = jnp.exp(jnp.where(causal[:, :, None], cum[:, :, :, None, :] - cum[:, :, None, :, :], -jnp.inf))
        scores = jnp.einsum('bhtk,bhsk,bhtsk->bhts', qc, kc, decay)
        intra = jnp.einsum('bhts,bhsv->bhtv', scores, vc)
        last = cum[:, :, -1:, :]
        new_state = jnp.exp(last[:, :, 0, :])[..., None] * state + jnp.einsum(
            'bhsk,bhsv->bhkv', kc * jnp.exp(last - cum), vc)
        return new_state, inter + intra

    s0 = jnp.zeros((b, h, dk, dv), jnp.float32)
    _, o = lax.scan(step, s0, (chunks(q), chunks(k), chunks(v), chunks(log_f)))
    return o.transpose(1, 0, 3, 2, 4).reshape(b, t, h, dv).astype(v.dtype)

def hybrid_mixer(h, layer, w_in, w_out, rel_bias, hgrn_lb, nsa_q_norm, nsa_k_norm, nsa_cmp_pos,
                 nsa_cmp_w1, nsa_cmp_w2, diff_q_norm, diff_k_norm, diff_lambda, diff_subln, hgrn_out_norm):
    b, t, _ = h.shape
    (nq, ck, cv, sk, sv, wk, wv, ng, dq, dk, dv, hq, hf, hi, hg) = split_cols(h @ w_in)

    def kvh(a):
        return a.reshape(b, t, NSA_KV_HEADS, HEAD_DIM)

    q_n = rms_norm(nq.reshape(b, t, NSA_HEADS, HEAD_DIM), nsa_q_norm)
    k_c = rms_norm(nsa_compress(kvh(ck), nsa_cmp_pos[0], nsa_cmp_w1[0], nsa_cmp_w2[0]), nsa_k_norm[0])
    v_c = nsa_compress(kvh(cv), nsa_cmp_pos[1], nsa_cmp_w1[1], nsa_cmp_w2[1])
    k_s = rms_norm(kvh(sk), nsa_k_norm[1])
    k_w = rms_norm(kvh(wk), nsa_k_norm[2])
    gates = jax.nn.sigmoid(ng.reshape(b, t, NSA_HEADS, 3))
    o_nsa = nsa_attention(q_n, k_c, v_c, k_s, kvh(sv), k_w, kvh(wv), gates, rel_bias[:, :NSA_HEADS])

    q_d = rms_norm(dq.reshape(b, t, DIFF_HEADS, 2, DIFF_QK_DIM), diff_q_norm)
    k_d = rms_norm(dk.reshape(b, t, DIFF_HEADS, 2, DIFF_QK_DIM), diff_k_norm)
    v_d = dv.reshape(b, t, DIFF_HEADS, HEAD_DIM)
    lam_init = 0.8 - 0.6 * math.exp(-0.3 * layer)
    lp = diff_lambda.astype(jnp.float32)
    lam = jnp.exp(jnp.sum(lp[0] * lp[1])) - jnp.exp(jnp.sum(lp[2] * lp[3])) + lam_init
    o_d = diff_attention(q_d, k_d, v_d, lam, rel_bias[:, NSA_HEADS:])
    o_d = rms_norm(o_d, diff_subln) * (1.0 - lam_init)

    fr = hf.reshape(b, t, HGRN_HEADS, HGRN_KEY_DIM).astype(jnp.float32)
    lb = hgrn_lb.reshape(HGRN_HEADS, HGRN_KEY_DIM)
    log_f = jnp.logaddexp(jnp.log(lb), jnp.log1p(-lb) + jax.nn.log_sigmoid(fr))
    i_gate = (1.0 - lb) * jax.nn.sigmoid(-fr)
    q_h = jax.nn.silu(hq.reshape(b, t, HGRN_HEADS, HGRN_KEY_DIM))
    o_h = hgrn2_scan(q_h, i_gate, hi.reshape(b, t, HGRN_HEADS, HGRN_VAL_DIM), log_f)
    o_h = rms_norm(o_h, hgrn_out_norm) * jax.nn.silu(hg.reshape(b, t, HGRN_HEADS, HGRN_VAL_DIM))

    mixed = jnp.concatenate([o_nsa, o_d.reshape(b, t, DIFF_WIDTH), o_h.reshape(b, t, HGRN_WIDTH)], axis=-1)
    return mixed @ w_out

def setup_inputs(seed: int = 0) -> dict:
    key = jax.random.key(seed)
    keys = iter(jax.random.split(key, 40))

    def normal(shape, scale):
        return jax.random.normal(next(keys), shape, jnp.float32) * scale

    def gain(shape):
        return 1.0 + 0.05 * jax.random.normal(next(keys), shape, jnp.float32)

    return {
        'x': normal((BATCH, SEQ, D_MODEL), 1.0),
        'p': normal((DEPTH, BATCH, SEQ, PLE_DIM), 1.0),
        'rel_bias': normal((NUM_BUCKETS, N_BIAS_HEADS), 0.2),
        'hgrn_lb_logits': normal((DEPTH, HGRN_KEY_WIDTH), 0.5),
        'ffn1_norm': gain((DEPTH, D_MODEL)),
        'ffn1_w_gate': normal((DEPTH, D_MODEL, D_FF), D_MODEL ** -0.5),
        'ffn1_w_up': normal((DEPTH, D_MODEL, D_FF), D_MODEL ** -0.5),
        'ffn1_w_down': normal((DEPTH, D_FF, D_MODEL), D_FF ** -0.5),
        'mix_norm': gain((DEPTH, D_MODEL)),
        'w_in': normal((DEPTH, D_MODEL, IN_WIDTH), D_MODEL ** -0.5),
        'w_out': normal((DEPTH, MIX_WIDTH, D_MODEL), MIX_WIDTH ** -0.5),
        'nsa_q_norm': gain((DEPTH, HEAD_DIM)),
        'nsa_k_norm': gain((DEPTH, 3, HEAD_DIM)),
        'nsa_cmp_pos': normal((DEPTH, 2, CMP_BLOCK, HEAD_DIM), 0.2),
        'nsa_cmp_w1': normal((DEPTH, 2, CMP_BLOCK * HEAD_DIM, CMP_HIDDEN), (CMP_BLOCK * HEAD_DIM) ** -0.5),
        'nsa_cmp_w2': normal((DEPTH, 2, CMP_HIDDEN, HEAD_DIM), CMP_HIDDEN ** -0.5),
        'diff_q_norm': gain((DEPTH, DIFF_QK_DIM)),
        'diff_k_norm': gain((DEPTH, DIFF_QK_DIM)),
        'diff_lambda': normal((DEPTH, 4, DIFF_QK_DIM), 0.1),
        'diff_subln': gain((DEPTH, HEAD_DIM)),
        'hgrn_out_norm': gain((DEPTH, HGRN_VAL_DIM)),
        'ffn2_norm': gain((DEPTH, D_MODEL)),
        'ffn2_w_gate': normal((DEPTH, D_MODEL, D_FF), D_MODEL ** -0.5),
        'ffn2_w_up': normal((DEPTH, D_MODEL, D_FF), D_MODEL ** -0.5),
        'ffn2_w_down': normal((DEPTH, D_FF, D_MODEL), D_FF ** -0.5),
        'ple_norm': gain((DEPTH, D_MODEL)),
        'ple_w_gate': normal((DEPTH, D_MODEL, D_MODEL), D_MODEL ** -0.5),
        'ple_w_proj': normal((DEPTH, PLE_DIM, D_MODEL), PLE_DIM ** -0.5),
        'ple_post_norm': gain((DEPTH, D_MODEL)),
    }

def reference(x, p, rel_bias, hgrn_lb_logits, ffn1_norm, ffn1_w_gate, ffn1_w_up, ffn1_w_down,
              mix_norm, w_in, w_out, nsa_q_norm, nsa_k_norm, nsa_cmp_pos, nsa_cmp_w1, nsa_cmp_w2,
              diff_q_norm, diff_k_norm, diff_lambda, diff_subln, hgrn_out_norm,
              ffn2_norm, ffn2_w_gate, ffn2_w_up, ffn2_w_down,
              ple_norm, ple_w_gate, ple_w_proj, ple_post_norm):
    lb_all = jnp.cumsum(jax.nn.softmax(hgrn_lb_logits.astype(jnp.float32), axis=0), axis=0)
    lb_all = lb_all - lb_all[0:1]
    for i in range(DEPTH):
        x = x + 0.5 * swiglu(rms_norm(x, ffn1_norm[i]), ffn1_w_gate[i], ffn1_w_up[i], ffn1_w_down[i])
        x = x + hybrid_mixer(rms_norm(x, mix_norm[i]), i, w_in[i], w_out[i], rel_bias, lb_all[i],
                             nsa_q_norm[i], nsa_k_norm[i], nsa_cmp_pos[i], nsa_cmp_w1[i], nsa_cmp_w2[i],
                             diff_q_norm[i], diff_k_norm[i], diff_lambda[i], diff_subln[i], hgrn_out_norm[i])
        x = x + 0.5 * swiglu(rms_norm(x, ffn2_norm[i]), ffn2_w_gate[i], ffn2_w_up[i], ffn2_w_down[i])
        gate = jax.nn.sigmoid(rms_norm(x, ple_norm[i]) @ ple_w_gate[i])
        x = x + gate * rms_norm(p[i] @ ple_w_proj[i], ple_post_norm[i])
    return x


_drawn_inputs = setup_inputs


def setup_inputs(seed=0):
    import zlib

    import numpy as np

    out = dict(_drawn_inputs(seed))
    spreads = {}
    factors = {'hgrn_lb_logits': 2.71,
     'nsa_q_norm': 8.0,
     'nsa_k_norm': 8.0,
     'diff_k_norm': 2.857,
     'diff_subln': 2.795,
     'hgrn_out_norm': 3.082,
     'ple_norm': 5.116}
    for name, (base, spread) in spreads.items():
        noise = np.random.default_rng([zlib.crc32(name.encode()), seed]).standard_normal(out[name].shape)
        drawn = base * np.exp(spread * noise) if base else spread * noise
        out[name] = jnp.asarray(drawn.astype(out[name].dtype))
    for name, factor in factors.items():
        out[name] = (out[name] * factor).astype(out[name].dtype)
    return out
```

```python
import math
from contextlib import ExitStack

import numpy as np

import concourse.bass as bass
from concourse import mybir
from concourse.alu_op_type import AluOpType as ALU

ACT = mybir.ActivationFunctionType
AX = mybir.AxisListType
F32 = mybir.dt.float32
F32R = mybir.dt.float32r
U32 = mybir.dt.uint32

P = 128
D_MODEL, SEQ, DEPTH, PLE_DIM, D_FF = 1024, 512, 2, 256, 2816
HEAD = 64
BUCKETS, MAX_DISTANCE = 32, 128
NEG = -1e30
EPS = 1e-6
NSA_HEADS, NSA_KV, GROUP = 6, 2, 3
CMP_BLOCK, CMP_STRIDE, CMP_HIDDEN = 32, 16, 256
NCMP = SEQ // CMP_STRIDE - 1
CPAD = 32
PAIRS = CMP_BLOCK // 2
DIFF_HEADS, DIFF_QK = 4, 32
HGRN_HEADS = 6
KT = D_MODEL // P
FT = D_FF // P
QT = SEQ // P
THIRDS = ((0, 8), (8, 15), (15, 22))
BIAS_HEADS = NSA_HEADS + DIFF_HEADS
LINE = P + SEQ
WIDE = KT * P
SLOTS = 3
AHEAD = 2
LEVELS = 9

_at = 0
COLS = {}
for _name, _n in (("ffn1", 8), ("mix", 8), ("ffn2", 8), ("ple", 8), ("post", 8), ("nq", 1), ("nk", 3), ("dq", 1),
                  ("dk", 1), ("subln", 1), ("hout", 1), ("lb", 6), ("lam", 128), ("pos", 32), ("flag", 1),
                  ("lam0", 1), ("sub0", 1)):
    COLS[_name] = (_at, _n)
    _at += _n
NCOLS = _at
NPARAM = COLS["flag"][0]

_at = 0
CONST = {}
for _name, _n in (("ident", 128), ("ones", 128), ("sum64", 128), ("sum32", 128), ("half", 2), ("quarter", 4),
                  ("cmask", QT * 2 * CPAD), ("live", 1), ("eps", 1), ("one", 1)):
    CONST[_name] = (_at, _n)
    _at += _n
NCONST = _at

_at = 0
SMALL = {}
for _name, _n in (("gq", 1), ("gdq", 1), ("gk", 4), ("gdk", 4), ("gsub", 1), ("nlam", 1), ("lam2", 64), ("e", 8),
                  ("max", 3), ("tot", 3), ("rec", 3), ("lb", 6), ("lc", 6), ("li", 6), ("ab", 6), ("rt", 4),
                  ("nm", 16), ("sum", 16), ("coef", 16), ("t01", 3), ("cmax", 24), ("csum", 24), ("ccoef", 24)):
    SMALL[_name] = (_at, _n)
    _at += _n
NSMALL = _at

TILES = ["hf0", "hf1", "hf2", "hq0", "hq1", "hq2", "ck", "cv", "sk", "wk", "nq0", "nq1", "nq2", "dk0", "dk1", "dq0",
         "dq1", "hg0", "hg1", "hg2"]
NORMED = ["sk", "wk", "nq0", "nq1", "nq2", "dk0", "dk1", "dq0", "dq1"]
GROUP_OF = {"C": TILES[0:6], "A": TILES[6:13], "B": TILES[13:20]}
NAT = {"C": 402, "A": 512}


def chunk_order():
    order = []
    for name in ("ffn1", "mix", "ffn2"):
        if name == "mix":
            for group in "CAB":
                order += [(tile,) for tile in GROUP_OF[group]]
                if group in NAT:
                    order += [("nat" + group, c) for c in range(4)]
            order += [("wout", dt) for dt in range(KT)]
            continue
        for ft in range(FT):
            order += [(name + "_gate", ft), (name + "_up", ft)]
        for dt in range(KT):
            order += [(name + "_down", dt, third) for third in range(3)]
    order += [("ple_proj", h) for h in range(2)]
    order += [("ple_gate", dt) for dt in range(KT)]
    return order


CHUNKS = chunk_order()
CHUNK = {key: n for n, key in enumerate(CHUNKS)}


def chunk_width(key):
    if key[0].startswith("nat"):
        return 2 * NAT[key[0][3]]
    if key[0].endswith("_down"):
        a, b = THIRDS[key[2]]
        return (b - a) * P
    return WIDE


def row0(i):
    return P * i * (i + 1) // 2


def col0(j):
    return P * (QT * j - j * (j - 1) // 2)


SCORES = row0(QT)


class Counts:

    def __init__(self, nc, ctx, known):
        self.nc, self.ctx, self.known = nc, ctx, known
        self.sems, self.n, self.seen, self.bank, self.frees = {}, {}, {}, {}, {}
        for kind in known.get("kinds", ()):
            self.sem(kind)

    def sem(self, kind):
        if kind not in self.sems:
            self.sems[kind] = self.ctx.enter_context(self.nc.semaphore(kind))
        return self.sems[kind]

    def tick(self, kind, *key, frees=None):
        self.n[kind] = self.n.get(kind, 0) + 1
        assert (kind, *key) not in self.seen, (kind, *key)
        self.seen[(kind, *key)] = self.n[kind]
        if frees is not None:
            assert frees not in self.frees, frees
            self.frees[frees] = (kind, *key)
        return self.sem(kind), 1

    def done(self, kind, *key):
        if not self.known:
            return self.sem(kind), 1
        return self.sem(kind), self.known["seen"][(kind, *key)]

    def freed(self, content):
        if not self.known:
            return self.sem("any"), 1
        return self.done(*self.known["frees"][content])

    def facts(self):
        return {"kinds": sorted(k for k in self.sems if k != "any"), "seen": self.seen, "frees": self.frees,
                "bank": self.bank}


def layers(nc, a, known):
    nc.disable_value_cache = True
    ctx = ExitStack()
    with ctx:
        def sem(name):
            return ctx.enter_context(nc.semaphore(name))

        place = {"at": 16512}

        def sb(name, shape, dt=F32):
            size = int(np.prod(shape[1:])) * 4
            t = nc.alloc_sbuf_tensor_at(name, shape, dt, offset=place["at"])
            place["at"] += (size + 31) // 32 * 32
            assert place["at"] <= 229344, (name, place["at"])
            return t

        x = sb("x_res", [P, KT, SEQ])
        xh, xl = sb("xh", [P, KT, SEQ], F32R), sb("xl", [P, KT, SEQ], F32R)
        raw = sb("raw", [P, SLOTS, WIDE])
        wh, wl = sb("wh", [P, SLOTS, WIDE], F32R), sb("wl", [P, SLOTS, WIDE], F32R)
        const = sb("const", [P, NCONST])
        lmask = sb("lmask", [P, 7, P])
        cols = sb("cols", [P, NCOLS])
        small = sb("small", [P, NSMALL])
        rb, acc = sb("rb", [P, SEQ]), sb("acc", [P, SEQ])
        sq = sb("sq", [P, 2, SEQ])
        region = place["at"]
        ffh, ffl = sb("ffh", [P, FT, SEQ], F32R), sb("ffl", [P, FT, SEQ], F32R)
        fg, fu = sb("fg", [P, 2, SEQ]), sb("fu", [P, 2, SEQ])
        place["at"] = region
        emb = sb("emb", [P, 2, SEQ])
        embh, embl = sb("embh", [P, 2, SEQ], F32R), sb("embl", [P, 2, SEQ], F32R)
        emby = sb("emby", [P, KT, SEQ])
        rb2 = sb("rb2", [P, SEQ])
        pg = sb("pg", [P, 2, SEQ])
        place["at"] = region
        mixed = sb("mixed", [P, KT, SEQ])
        gates = sb("gates", [P, QT, 18])
        z = sb("z", [P, 3, SEQ])
        zs = sb("zs", [P, 2, SEQ])
        rn = sb("rn", [P, SEQ])
        group0 = place["at"]
        hf, hq = sb("hf", [P, 3, SEQ]), sb("hq", [P, 3, SEQ])
        hv = sb("hv", [P, QT, 3, 4, HEAD])
        cum = sb("cum", [P, 3, SEQ])
        ev, zv = sb("ev", [P, 2, SEQ]), sb("zv", [P, 2, SEQ])
        hgrn_tmp = place["at"]
        sdiag, soff = sb("sdiag", [P, 2, SEQ]), sb("soff", [P, 2, 6 * P])
        place["at"] = hgrn_tmp
        ta, tb, tc = sb("ta", [P, SEQ]), sb("tb", [P, SEQ]), sb("tc", [P, SEQ])
        hgrn_end = hgrn_tmp + 4 * (2 * SEQ + 12 * P)
        place["at"] = group0
        dv = sb("dv", [P, QT, 2, 4, HEAD])
        q = sb("q", [P, 3, SEQ])
        kpad = sb("kpad", [P, 2, NSA_KV, SEQ])
        vpad = sb("vpad", [P, 2, QT, 4, HEAD])
        kc, vc = sb("kc", [P, 2 * CPAD]), sb("vc", [P, P])
        cp = sb("cp", [P, 12, 2 * CPAD])
        ckv = sb("ckv", [P, 2, SEQ])
        stage0 = place["at"]
        c2 = sb("c2", [P, 2, 2, SEQ])
        w2c = sb("w2c", [P, PAIRS, 2 * NCMP])
        w1 = sb("w1", [P, 2, 4, CMP_HIDDEN])
        w2s = sb("w2s", [P, 2, 2, HEAD])
        w2p = sb("w2p", [P, 2, 2, 3, HEAD])
        hid = sb("hid", [P, CMP_HIDDEN])
        hidT = sb("hidT", [P, 2, 2 * NCMP])
        place["at"] = stage0
        biasA = sb("biasA", [P, NSA_HEADS, SEQ])
        probs = sb("probs", [P, 2, SCORES])
        probsT = sb("probsT", [P, 2, SCORES])
        place["at"] = group0 + 4 * QT * 2 * 4 * HEAD
        dq = sb("dqt", [P, 2, SEQ])
        dkp = sb("dkp", [P, 2, 4, SEQ])
        biasB = sb("biasB", [P, DIFF_HEADS, SEQ])
        dp = sb("dp", [P, 2, 2, SCORES])
        dpT = sb("dpT", [P, SCORES])
        place["at"] = region
        tab = sb("tab", [P, BIAS_HEADS])
        onehot = sb("onehot_sb", [P, LINE])
        line = sb("line", [P, LINE])

        main = [ctx.enter_context(nc.psum_tensor(f"main{b}", [P, SEQ], F32)) for b in range(4)]
        side = [ctx.enter_context(nc.psum_tensor(f"side{b}", [P, SEQ], F32)) for b in range(4)]
        lines = nc.dram_tensor("bias_lines", [BIAS_HEADS, P, LINE], F32).ap()

        def const_(name):
            at, n = CONST[name]
            return const[:, at:at + n]

        def col(name, k=0, n=1):
            at = COLS[name][0] + k
            return cols[:, at:at + n]

        def sm(name, k=0, n=1):
            at = SMALL[name][0] + k
            return small[:, at:at + n]

        const_in, x_in, tab_ready, line_made, line_read, line_out, x_out = (
            sem(n) for n in ("const_in", "x_in", "tab_ready", "line_made", "line_read", "line_out", "x_out"))
        with nc.Block() as block:
            @block.sync
            def _(sp):
                sp.dma_start(const[:], a["consts"]).then_inc(const_in, 16)
                sp.dma_start(lmask[:], a["level_masks"]).then_inc(const_in, 16)
                sp.dma_start(onehot[0:33, :], a["onehot"]).then_inc(const_in, 16)
                sp.dma_start(tab[0:BUCKETS, :], a["rel_bias"]).then_inc(const_in, 16)
                sp.dma_start(x[:], a["x"]).then_inc(x_in, 16)
                sp.wait_ge(line_read, 2)
                sp.dma_start(lines, line[0:BIAS_HEADS, None, :].broadcast_to([BIAS_HEADS, P, LINE])
                             ).then_inc(line_out, 16)
                sp.wait_ge(line_out, 16)
                sp.wait_ge(x_in, 16)

            @block.gpsimd
            def _(pool):
                nc.gpsimd.memset(tab[BUCKETS:BUCKETS + 1, :], NEG).then_inc(tab_ready, 1)

            @block.tensor
            def _(pe):
                pe.wait_ge(const_in, 64)
                pe.wait_ge(tab_ready, 1)
                nc.tensor.matmul(side[0][0:BIAS_HEADS, :], tab[0:33, :], onehot[0:33, 0:SEQ], start=True, stop=True)
                nc.tensor.matmul(side[1][0:BIAS_HEADS, 0:P], tab[0:33, :], onehot[0:33, SEQ:LINE], start=True,
                                 stop=True).then_inc(line_made, 1)

            @block.vector
            def _(dve):
                dve.wait_ge(line_made, 1)
                nc.vector.tensor_copy(line[0:BIAS_HEADS, 0:SEQ], side[0][0:BIAS_HEADS, :]).then_inc(line_read, 1)
                nc.vector.tensor_copy(line[0:BIAS_HEADS, SEQ:LINE],
                                      side[1][0:BIAS_HEADS, 0:P]).then_inc(line_read, 1)

        def bias_lines(head, n):
            return bass.AP(lines.tensor, head * P * LINE + P - 1, [[LINE - 1, P], [P * LINE, n], [1, SEQ]])

        raw_full = [sem(f"raw_full{b}") for b in range(SLOTS)]
        params_in, w2_in, emb_in = (sem(n) for n in ("params_in", "w2_in", "emb_in"))
        w1_in = [sem("w1_in0"), sem("w1_in1")]
        shift_in = [sem("shift_in_keys"), sem("shift_in_values")]
        bias_in = [sem("bias_in_nsa"), sem("bias_in_diff")]
        cleared = [*raw_full, params_in, w2_in, emb_in, *w1_in, *shift_in, *bias_in]
        counts = Counts(nc, ctx, known)
        tick, done, freed = counts.tick, counts.done, counts.freed

        def bank_of(content):
            if not known:
                return main[0]
            which, n = known["bank"][content]
            return (main, side)[which][n % 4]

        def source(key, layer):
            if key[0] in TILES:
                return a["w_in_t"][layer, TILES.index(key[0])]
            if key[0].endswith("_down"):
                lo, hi = THIRDS[key[2]]
                return a[key[0]][layer, key[1], :, lo * P:hi * P]
            return a[key[0]][layer, key[1]]

        with nc.Fori(0, DEPTH) as layer:
            with nc.Block() as block:
                @block.sync
                def _(sp):
                    sp.dma_start(cols[:, 0:NPARAM], a["params"][layer]).then_inc(params_in, 16)
                    sp.dma_start(cols[:, NPARAM:NCOLS], a["layer_consts"][layer]).then_inc(params_in, 16)
                    for c, key in enumerate(CHUNKS):
                        if c >= SLOTS:
                            sp.wait_ge(*done("weights_lo", c - SLOTS))
                        sp.dma_start(raw[:, c % SLOTS, 0:chunk_width(key)],
                                     source(key, layer)).then_inc(raw_full[c % SLOTS], 16)

                @block.gpsimd
                def _(pool):
                    pool.wait_ge(*done("product", ("ffn1_down", KT - 1, 2)))
                    pool.wait_ge(*done("h_lo", "ffn1", FT - 1))
                    nc.gpsimd.memset(hv[:], 0.0).then_inc(*tick("zeros", "hv"))
                    for p in range(3):
                        for lev in range(LEVELS):
                            g = p * LEVELS + lev
                            pool.wait_ge(*done("decay", p, lev))
                            if g == 0:
                                pool.wait_ge(*done("q_silu"))
                            if lev == 0:
                                pool.wait_ge(*done("hgrn_k", p))
                            if g >= 2:
                                pool.wait_ge(*done("hgrn_scores", g - 2, 1))
                            size = 1 << lev
                            e, o = ev[:, g % 2, :], zv[:, g % 2, :]
                            cut = "p (b two l) -> p b two l"
                            for which, operand in ((0, hf[:, p, :]), (1, hq[:, p, :])):
                                nc.gpsimd.tensor_tensor(
                                    o.rearrange(cut, two=2, l=size)[:, :, which, :],
                                    e.rearrange(cut, two=2, l=size)[:, :, which, :],
                                    operand.rearrange(cut, two=2, l=size)[:, :, which, :],
                                    ALU.mult).then_inc(*tick("decayed", g, which))
                    pool.wait_ge(*done("hgrn_out", 2))
                    nc.gpsimd.memset(vpad[:], 0.0).then_inc(*tick("zeros", "vpad"))
                    nc.gpsimd.memset(dv[:], 0.0).then_inc(*tick("zeros", "dv"))
                    nc.gpsimd.memset(w2p[:], 0.0).then_inc(*tick("zeros", "w2p"))
                    nc.gpsimd.memset(kc[:], 0.0).then_inc(*tick("zeros", "kc"))
                    nc.gpsimd.memset(vc[:], 0.0).then_inc(*tick("zeros", "vc"))

                @block.tensor
                def _(pe):
                    taken = {0: [], 1: []}

                    def take(content, which=1):
                        order = taken[which]
                        n = len(order)
                        if n >= 4:
                            pe.wait_ge(*freed(order[n - 4]))
                        order.append(content)
                        counts.bank[content] = (which, n)
                        return (main, side)[which][n % 4]

                    def three(out, lh, ll, rh, rl, start, stop, **kw):
                        nc.tensor.matmul(out, lh, rh, start=start, stop=False, **kw)
                        nc.tensor.matmul(out, lh, rl, start=False, stop=False, **kw)
                        return nc.tensor.matmul(out, ll, rh, start=False, stop=stop, **kw)

                    def chunk(key):
                        c, n = CHUNK[key], chunk_width(key)
                        pe.wait_ge(*done("weights_lo", c))
                        return wh[:, c % SLOTS, 0:n], wl[:, c % SLOTS, 0:n]

                    def from_x(key, stage=None):
                        out = take(key, 0)
                        h, l = chunk(key)
                        for k in range(KT):
                            if stage:
                                pe.wait_ge(*done("x_lo", stage, k))
                            ks = slice(k * P, (k + 1) * P)
                            mm = three(out[:], h[:, ks], l[:, ks], xh[:, k, :], xl[:, k, :], k == 0, k == KT - 1)
                        mm.then_inc(*tick("product", key))

                    def sum_squares(name):
                        out = take(("squares", name))
                        pe.wait_ge(*done("squares_added", name, KT - 1))
                        nc.tensor.matmul(out[:], const_("ones"), acc[:], start=True,
                                         stop=True).then_inc(*tick("squares", name))

                    def head_squares(name, blocks, rhs, n=SEQ):
                        out = take(("head_squares", name))
                        pe.wait_ge(*done("head_sq", name))
                        nc.tensor.matmul(out[:, 0:n], const_(blocks), rhs, start=True,
                                         stop=True).then_inc(*tick("head_squares", name))

                    def ffn(name):
                        for ft in range(FT):
                            from_x((name + "_gate", ft), name if ft == 0 else None)
                            if ft == 0:
                                sum_squares(name)
                            from_x((name + "_up", ft))
                        for dt in range(KT):
                            out = take((name + "_down", dt), 0)
                            for third, (lo, hi) in enumerate(THIRDS):
                                key = (name + "_down", dt, third)
                                h, l = chunk(key)
                                for f in range(lo, hi):
                                    if dt == 0:
                                        pe.wait_ge(*done("h_lo", name, f))
                                    fs = slice((f - lo) * P, (f - lo + 1) * P)
                                    mm = three(out[:], h[:, fs], l[:, fs], ffh[:, f, :], ffl[:, f, :], f == 0,
                                               f == FT - 1)
                                if third < 2:
                                    mm.then_inc(*tick("product", key))
                            mm.then_inc(*tick("product", key))

                    def project(group):
                        names = GROUP_OF[group]
                        for j, name in enumerate(names):
                            from_x((name,), "mix" if name == TILES[0] else None)
                            if name == TILES[0]:
                                sum_squares("mix")
                            if name == TILES[1]:
                                out = take("turned")
                                pe.wait_ge(*done("factor", "mix"))
                                for t in range(QT):
                                    ts = slice(t * P, (t + 1) * P)
                                    mm = nc.tensor.transpose(out[:, ts], rb[:, ts], const_("ident"))
                                mm.then_inc(*tick("turned"))
                            if j and names[j - 1] in NORMED:
                                norm(names[j - 1])
                        if group in NAT:
                            w = NAT[group]
                            outs = [take(("nat" + group, t, "out"), 0) for t in range(QT)]
                            for c in range(4):
                                h, l = chunk(("nat" + group, c))
                                for t in range(QT):
                                    ts = slice(t * P, (t + 1) * P)
                                    for kk in range(2):
                                        k, ks = 2 * c + kk, slice(kk * w, (kk + 1) * w)
                                        mm = three(outs[t][:, 0:w], xh[:, k, ts], xl[:, k, ts], h[:, ks], l[:, ks],
                                                   k == 0, k == KT - 1)
                                mm.then_inc(*tick("product", ("nat" + group, c)))
                        if names[-1] in NORMED:
                            norm(names[-1])

                    def norm(name):
                        k = NORMED.index(name)
                        head_squares(name, "sum32" if name[0] == "d" else "sum64", zs[:, k % 2, :])

                    def hgrn():
                        for p in range(3):
                            for lev in range(-1, LEVELS):
                                g = p * LEVELS + lev
                                if lev < 0:
                                    pe.wait_ge(*done("q_silu"))
                                    pe.wait_ge(*done("hgrn_k", p))
                                else:
                                    pe.wait_ge(*done("decayed", g, 1))
                                for hh in range(2):
                                    out = take(("h", p, lev, hh))
                                    rows = slice(64 * hh, 64 * hh + 64)
                                    first = hf[rows, p, :] if lev < 0 else zv[rows, g % 2, :]
                                    second = hq[rows, p, :] if lev < 0 else zv[rows, g % 2, :]
                                    if lev < 7:
                                        parts = [(t * P, t * P, t * P, P) for t in range(QT)]
                                    elif lev == 7:
                                        parts = [(t * P, 2 * t * P, (2 * t + 1) * P, P) for t in range(2)]
                                    else:
                                        parts = [(2 * t * P, t * P, 2 * P, 2 * P) for t in range(2)]
                                    for o, s, t, w in parts:
                                        mm = nc.tensor.matmul(out[:, o:o + w], first[:, s:s + P], second[:, t:t + w],
                                                              start=True, stop=True)
                                    mm.then_inc(*(tick("hgrn_scores", g, hh) if lev >= 0 else
                                                  tick("hgrn_same", p, hh)))
                            out = take(("hgrn", p), 0)
                            pe.wait_ge(*freed(("h", p, 6, 1)))
                            pe.wait_ge(*freed(("h", p, 8, 1)))
                            for hh in range(2):
                                for j in range(QT):
                                    v = hv[:, j, p, 2 * hh:2 * hh + 2, :].rearrange("p a d -> p (a d)")
                                    mm = nc.tensor.matmul(out[:, j * P:(j + 1) * P], v,
                                                          sdiag[:, hh, j * P:(j + 1) * P],
                                                          start=(hh == 0 and j == 0),
                                                          stop=False, skip_group_check=True)
                                    if j < QT - 1:
                                        o = (0, 3, 5)[j] * P
                                        mm = nc.tensor.matmul(out[:, (j + 1) * P:SEQ], v,
                                                              soff[:, hh, o:o + (QT - 1 - j) * P], start=False,
                                                              stop=False, skip_group_check=True)
                            mm.then_inc(*tick("hgrn_values", p))
                            head_squares(("hgrn", p), "sum64", zs[:, p % 2, :])

                    def compress():
                        n2 = 2 * NCMP
                        for kv in range(2):
                            out = take(("hidden", kv))
                            pe.wait_ge(*done("windows", kv))
                            for m in range(PAIRS):
                                k = 4 * kv + m // 4
                                if m % 4 == 0:
                                    pe.wait_ge(w1_in[k % 2], 16 * (k // 2 + 1))
                                mm = nc.tensor.matmul(out[0:n2, 0:CMP_HIDDEN], w2c[:, m, :], w1[:, k % 2, m % 4, :],
                                                      start=(m == 0), stop=(m == PAIRS - 1))
                                if m % 4 == 3:
                                    mm.then_inc(*tick("cmp_part", k))
                            out = take(("hiddenT", kv))
                            pe.wait_ge(*done("cmp_gelu", kv))
                            for k in range(2):
                                mm = nc.tensor.transpose(out[:, k * n2:(k + 1) * n2], hid[0:n2, k * P:(k + 1) * P],
                                                         const_("ident")[0:n2, 0:n2])
                            mm.then_inc(*tick("cmp_turned", kv))
                            out = take(("compressed", kv))
                            pe.wait_ge(*freed(("hiddenT", kv)))
                            pe.wait_ge(*done("w2_padded", kv))
                            for g in range(2):
                                for k in range(2):
                                    pad = w2p[:, kv, k, 1 - g:3 - g, :].rearrange("p a d -> p (a d)")
                                    part = hidT[:, k, g * NCMP:(g + 1) * NCMP]
                                    if kv == 0:
                                        mm = nc.tensor.matmul(out[:, CPAD * g:CPAD * g + NCMP], pad, part,
                                                              start=(k == 0), stop=(k == 1))
                                    else:
                                        mm = nc.tensor.matmul(out[CPAD * g:CPAD * g + NCMP, 0:P], part, pad,
                                                              start=(k == 0), stop=(k == 1))
                            mm.then_inc(*tick("cmp_made", kv))
                            if kv == 0:
                                head_squares("kc", "sum64", zs[:, 1, 0:2 * CPAD], n=2 * CPAD)

                    def compressed_scores():
                        pe.wait_ge(*done("kc"))
                        pe.wait_ge(*done("normed", "nq2", 0))
                        for part, rs in enumerate(((0, 1), (2,))):
                            out = take(("cmp_scores", part))
                            for n, (r, i) in enumerate((r, i) for r in rs for i in range(QT)):
                                mm = nc.tensor.matmul(out[:, n * 2 * CPAD:(n + 1) * 2 * CPAD],
                                                      q[:, r, i * P:(i + 1) * P], kc[:], start=True, stop=True)
                            mm.then_inc(*tick("cmp_scores", part))
                        pe.wait_ge(*done("cmp_probs"))
                        for r in range(3):
                            out = take(("cmp_turn", r))
                            for i in range(QT):
                                mm = nc.tensor.transpose(out[0:2 * CPAD, i * P:(i + 1) * P], cp[:, r * QT + i, :],
                                                         const_("ident"))
                            mm.then_inc(*tick("cmp_probsT", r))

                    def nsa():
                        outs = {}
                        for n in range(14):
                            if n < 12:
                                r, g, b = n // 4, n // 2 % 2, n % 2
                                for i in range(QT):
                                    out = take(("s", n, i))
                                    nc.tensor.matmul(out[:, 0:(i + 1) * P], q[:, r, i * P:(i + 1) * P],
                                                     kpad[:, b, g, 0:(i + 1) * P], start=True,
                                                     stop=True).then_inc(*tick("scores", n, i))
                                if n % 4 == 0:
                                    outs[r] = take(("nsa", r), 0)
                                    pe.wait_ge(*freed(("cmp_turn", r)))
                                    pe.wait_ge(*done("vc", 1))
                                    nc.tensor.matmul(outs[r][:], vc[0:2 * CPAD, :], mixed[0:2 * CPAD, r, :],
                                                     start=True, stop=False, skip_group_check=True)
                            if n >= 2:
                                m = n - 2
                                r, g, b = m // 4, m // 2 % 2, m % 2
                                for j in range(QT):
                                    pe.wait_ge(*freed(("t", m, j)))
                                    v = vpad[:, b, j, 2 * g:2 * g + 2, :].rearrange("p a d -> p (a d)")
                                    mm = nc.tensor.matmul(outs[r][:, j * P:SEQ], v,
                                                          probsT[:, m % 2, col0(j):col0(j + 1)], start=False,
                                                          stop=False, skip_group_check=True)
                                mm.then_inc(*tick("values_used", m))
                            if 1 <= n <= 12:
                                m = n - 1
                                for j in range(QT):
                                    out = take(("t", m, j))
                                    pe.wait_ge(*done("probs_scaled", m, QT - 1))
                                    for i in range(j, QT):
                                        at = row0(i) + j * P
                                        mm = nc.tensor.transpose(out[:, i * P:(i + 1) * P],
                                                                 probs[:, m % 2, at:at + P], const_("ident"))
                                    mm.then_inc(*tick("turned_probs", m, j))

                    def diff():
                        outs = {}
                        for n in range(DIFF_HEADS + 2):
                            if n < DIFF_HEADS:
                                for m in range(2):
                                    for i in range(QT):
                                        out = take(("ds", n, m, i))
                                        nc.tensor.matmul(out[:, 0:(i + 1) * P], dq[:, n // 2, i * P:(i + 1) * P],
                                                         dkp[:, n // 2, 2 * (n % 2) + m, 0:(i + 1) * P], start=True,
                                                         stop=True).then_inc(*tick("dscores", n, m, i))
                                if n % 2 == 0:
                                    outs[n // 2] = take(("diff", n // 2), 0)
                            if n >= 2:
                                d = n - 2
                                for j in range(QT):
                                    pe.wait_ge(*freed(("dt", d, j)))
                                    v = dv[:, j, d // 2, 2 * (d % 2):2 * (d % 2) + 2, :].rearrange("p a d -> p (a d)")
                                    mm = nc.tensor.matmul(outs[d // 2][:, j * P:SEQ], v,
                                                          dpT[:, col0(j):col0(j + 1)],
                                                          start=(d % 2 == 0 and j == 0), stop=False,
                                                          skip_group_check=True)
                                mm.then_inc(*tick("dvalues_used", d))
                            if 1 <= n <= DIFF_HEADS:
                                d = n - 1
                                for j in range(QT):
                                    out = take(("dt", d, j))
                                    pe.wait_ge(*done("dprobs", d, QT - 1))
                                    for i in range(j, QT):
                                        at = row0(i) + j * P
                                        mm = nc.tensor.transpose(out[:, i * P:(i + 1) * P], dp[:, d % 2, 0, at:at + P],
                                                                 const_("ident"))
                                    mm.then_inc(*tick("dturned_probs", d, j))
                        for t in range(2):
                            head_squares(("diff", t), "sum64", zs[:, t, :])

                    ffn("ffn1")
                    project("C")
                    hgrn()
                    project("A")
                    compress()
                    compressed_scores()
                    nsa()
                    project("B")
                    diff()
                    for dt in range(KT):
                        from_x(("wout", dt), "mixed" if dt == 0 else None)
                    ffn("ffn2")
                    for h2 in range(2):
                        key = ("ple_proj", h2)
                        h, l = chunk(key)
                        pe.wait_ge(*done("emb_lo", 1))
                        for d in range(4):
                            out = take(("ple_out", 4 * h2 + d), 0)
                            for k in range(2):
                                ks = slice((2 * d + k) * P, (2 * d + k + 1) * P)
                                mm = three(out[:], h[:, ks], l[:, ks], embh[:, k, :], embl[:, k, :], k == 0, k == 1)
                            mm.then_inc(*(tick("product", key) if d == 3 else tick("product", key, d)))
                        sum_squares(("ple", "post")[h2])
                    for dt in range(KT):
                        from_x(("ple_gate", dt), "ple" if dt == 0 else None)

                @block.scalar
                def _(act):
                    at = {"hi": 0}

                    def split(upto):
                        while at["hi"] <= min(upto, len(CHUNKS) - 1):
                            c = at["hi"]
                            n = chunk_width(CHUNKS[c])
                            act.wait_ge(raw_full[c % SLOTS], 16 * (c // SLOTS + 1))
                            if c >= SLOTS:
                                act.wait_ge(*done("product", CHUNKS[c - SLOTS]))
                            nc.scalar.activation(wh[:, c % SLOTS, 0:n], raw[:, c % SLOTS, 0:n],
                                                 ACT.Copy).then_inc(*tick("weights_hi", c))
                            at["hi"] += 1

                    def split_x(stage, gain, k):
                        nc.scalar.activation(xh[:, k, :], x[:, k, :], ACT.Identity, bias=0.0,
                                             scale=col(gain, k)).then_inc(*tick("x_hi", stage, k))

                    def square(norm, k, operand):
                        n = NORMS.index(norm) * KT + k
                        if n >= 2:
                            m = n - 2
                            act.wait_ge(*done("squares_added", NORMS[m // KT], max(m % KT, 1)))
                        nc.scalar.activation(sq[:, k % 2, :], operand,
                                             ACT.Square).then_inc(*tick("squared", norm, k))

                    def factor(name, out):
                        act.wait_ge(*done("squares", name))
                        nc.scalar.activation(out, bank_of(("squares", name))[:], ACT.Ln, bias=const_("eps"),
                                             scale=1.0 / D_MODEL).then_inc(
                                                 *tick("factor_ln", name, frees=("squares", name)))
                        act.wait_ge(*done("factor_ln", name))
                        nc.scalar.activation(out, out, ACT.Exp, scale=-0.5).then_inc(*tick("factor", name))

                    def head_factor(name, width, n=SEQ):
                        key = ("head_squares", name)
                        act.wait_ge(*done(*key))
                        if RN_BEFORE[name] is not None:
                            act.wait_ge(*done(*RN_BEFORE[name]))
                        nc.scalar.activation(rn[:, 0:n], bank_of(key)[:, 0:n], ACT.Ln, bias=const_("eps"),
                                             scale=1.0 / width).then_inc(*tick("head_ln", name, frees=key))
                        act.wait_ge(*done("head_ln", name))
                        nc.scalar.activation(rn[:, 0:n], rn[:, 0:n], ACT.Exp,
                                             scale=-0.5).then_inc(*tick("head_factor", name))

                    def ffn(name, nxt, gain, last_user):
                        for ft in range(FT + 1):
                            if ft < FT:
                                c = CHUNK[(name + "_gate", ft)]
                                split(c + AHEAD)
                                if ft == 0:
                                    factor(name, rb[:])
                                act.wait_ge(*done("gate_scaled", name, ft))
                                nc.scalar.activation(fg[:, ft % 2, :], fg[:, ft % 2, :],
                                                     ACT.Silu).then_inc(*tick("gate_silu", name, ft))
                                split(c + 1 + AHEAD)
                            if ft:
                                act.wait_ge(*done("h", name, ft - 1))
                                nc.scalar.activation(ffh[:, ft - 1, :], fu[:, (ft - 1) % 2, :],
                                                     ACT.Copy).then_inc(*tick("h_hi", name, ft - 1))
                            if name == "ffn1" and ft == 1:
                                act.wait_ge(*done("exponents"))
                                nc.scalar.activation(sm("e", 0, 8), sm("e", 0, 8),
                                                     ACT.Exp).then_inc(*tick("exponentials"))
                                act.wait_ge(*done("logarithm_of"))
                                nc.scalar.activation(sm("lc", 0, 6), sm("lc", 0, 6),
                                                     ACT.Ln).then_inc(*tick("logarithms"))
                        for dt in range(KT):
                            for third in range(3):
                                split(CHUNK[(name + "_down", dt, third)] + AHEAD)
                            act.wait_ge(*done("x_new", name, dt))
                            split_x(nxt, gain, dt)
                            square(nxt, dt, x[:, dt, :])

                    def project(group):
                        names = GROUP_OF[group]
                        for j, name in enumerate(names):
                            split(CHUNK[(name,)] + AHEAD)
                            if name == TILES[0]:
                                factor("mix", rb[:])
                            if name == "sk":
                                shift_pairs()
                            if name in NORMED:
                                k = NORMED.index(name)
                                act.wait_ge(*done("scaled", name))
                                if k >= 2:
                                    act.wait_ge(*done("head_squares", NORMED[k - 2]))
                                nc.scalar.activation(zs[:, k % 2, :], z[:, TILES.index(name) % 3, :],
                                                     ACT.Square).then_inc(*tick("head_sq", name))
                            if name[:2] == "hg":
                                act.wait_ge(*done("scaled", name))
                                zz = z[:, TILES.index(name) % 3, :]
                                nc.scalar.activation(zz, zz, ACT.Silu).then_inc(*tick("out_gate", name))
                            if j and names[j - 1] in NORMED:
                                head_factor(names[j - 1], DIFF_QK if names[j - 1][0] == "d" else HEAD)
                        if group in NAT:
                            for c in range(4):
                                split(CHUNK[("nat" + group, c)] + AHEAD)
                            act.wait_ge(*done("product", ("nat" + group, 3)))
                            act.wait_ge(*done("factor_turned"))
                            act.wait_ge(*done("zeros", "hv" if group == "C" else "dv"))
                            for t in range(QT):
                                key = ("nat" + group, t, "out")
                                o = bank_of(key)

                                def heads(n):
                                    return o[:, n * P:(n + 1) * P].rearrange("p (g d) -> p g d", g=2)

                                if group == "C":
                                    for p in range(3):
                                        nc.scalar.activation(hv[:, t, p, 0:4:3, :], heads(p), ACT.Copy,
                                                             scale=sm("rt", t)).then_inc(*tick("values", "C", t, p))
                                    nc.scalar.activation(gates[:, t, :], o[:, 384:402], ACT.Copy,
                                                         scale=sm("rt", t)).then_inc(
                                                             *tick("values", "C", t, 3, frees=key))
                                else:
                                    for b in range(2):
                                        nc.scalar.activation(vpad[:, b, t, 0:4:3, :], heads(b), ACT.Copy,
                                                             scale=sm("rt", t)).then_inc(*tick("values", "A", t, b))
                                    for b in range(2):
                                        nc.scalar.activation(dv[:, t, b, 0:4:3, :], heads(2 + b), ACT.Copy,
                                                             scale=sm("rt", t)).then_inc(
                                            *tick("values", "A", t, 2 + b, frees=key if b else None))
                            if group == "C":
                                act.wait_ge(*done("values", "C", QT - 1, 3))
                                nc.scalar.activation(gates[:], gates[:], ACT.Exp,
                                                     scale=-1.0).then_inc(*tick("gate_exp"))
                        if names[-1] in NORMED:
                            head_factor(names[-1], DIFF_QK if names[-1][0] == "d" else HEAD)

                    def hgrn():
                        act.wait_ge(*done("scaled", "hq2"))
                        nc.scalar.activation(hq[:], hq[:], ACT.Silu).then_inc(*tick("q_silu"))
                        for p in range(3):
                            if p:
                                act.wait_ge(*done("log_forget", p - 1))
                            f = hf[:, p, :]
                            nc.scalar.activation(ta[:], f, ACT.Abs).then_inc(*tick("forget", p, 0))
                            act.wait_ge(*done("forget", p, 0))
                            nc.scalar.activation(ta[:], ta[:], ACT.Exp, scale=-1.0).then_inc(*tick("forget", p, 1))
                            act.wait_ge(*done("forget", p, 1))
                            nc.scalar.activation(ta[:], ta[:], ACT.Ln,
                                                 bias=const_("one")).then_inc(*tick("forget", p, 2))
                            act.wait_ge(*done("log_gap", p))
                            nc.scalar.activation(tb[:], tb[:], ACT.Abs).then_inc(*tick("forget", p, 3))
                            act.wait_ge(*done("forget", p, 3))
                            nc.scalar.activation(tb[:], tb[:], ACT.Exp, scale=-1.0).then_inc(*tick("forget", p, 4))
                            act.wait_ge(*done("forget", p, 4))
                            nc.scalar.activation(tb[:], tb[:], ACT.Ln,
                                                 bias=const_("one")).then_inc(*tick("forget", p, 5))
                            act.wait_ge(*done("log_input", p))
                            nc.scalar.activation(f, f, ACT.Exp).then_inc(*tick("forget", p, 6))
                        for p in range(3):
                            for lev in range(LEVELS):
                                g = p * LEVELS + lev
                                e = ev[:, g % 2, :]
                                if lev < 7:
                                    act.wait_ge(*done("exponent", g, 1))
                                    nc.scalar.activation(e, e, ACT.Exp).then_inc(*tick("decay", p, lev))
                                    continue
                                act.wait_ge(*done("cumsum", p, "t01"))
                                if g >= 2:
                                    act.wait_ge(*done("decayed", g - 2, 1))
                                c = cum[:, p, :]
                                tot = [cum[:, p, (t + 1) * P - 1:(t + 1) * P] for t in range(QT)]
                                before = {0: tot[0], 2: tot[2]} if lev == 7 else {0: sm("t01", p), 1: tot[1]}
                                behind = {1: 0.0, 3: 0.0} if lev == 7 else {2: 0.0, 3: tot[2]}
                                for t in range(QT):
                                    ts = slice(t * P, (t + 1) * P)
                                    if t in before:
                                        ins = nc.scalar.activation(e[:, ts], c[:, ts], ACT.Exp, bias=before[t],
                                                                   scale=-1.0)
                                    else:
                                        ins = nc.scalar.activation(e[:, ts], c[:, ts], ACT.Exp, bias=behind[t])
                                    ins.then_inc(*(tick("decay", p, lev) if t == QT - 1 else
                                                   tick("decay", p, lev, t)))
                            for lev, parts in ((7, ((0, 0, 1), (5, 1, 2))), (8, ((1, 0, 2), (3, 2, 4)))):
                                for hh in range(2):
                                    key = ("h", p, lev, hh)
                                    act.wait_ge(*done("hgrn_scores", p * LEVELS + lev, hh))
                                    if p:
                                        act.wait_ge(*done("hgrn_values", p - 1))
                                    else:
                                        act.wait_ge(*done("log_forget", 2))
                                    for n, (to, lo, hi) in enumerate(parts):
                                        nc.scalar.activation(
                                            soff[:, hh, to * P:(to + hi - lo) * P], bank_of(key)[:, lo * P:hi * P],
                                            ACT.Copy).then_inc(*tick("far_scores", p, lev, hh, n,
                                                                     frees=key if n else None))
                            act.wait_ge(*done("hgrn_values", p))
                            if p:
                                act.wait_ge(*done("hgrn_out", p - 1))
                            nc.scalar.activation(zs[:, p % 2, :], bank_of(("hgrn", p))[:],
                                                 ACT.Square).then_inc(*tick("head_sq", ("hgrn", p)))
                            head_factor(("hgrn", p), HEAD)

                    def load_w1(k):
                        act.dma_start(w1[:, k % 2], a["cmp_w1"][layer, k // 4, k % 4]).then_inc(w1_in[k % 2], 16)

                    def load_compression():
                        act.wait_ge(*done("hgrn_out", 2))
                        act.dma_start(w2s[:], a["cmp_w2"][layer]).then_inc(w2_in, 16)
                        for k in range(2):
                            load_w1(k)

                    def shift_pairs():
                        for kv, name in enumerate(("ck", "cv")):
                            act.wait_ge(*done("scaled", name))
                            for head in range(2):
                                for odd in range(2):
                                    act.dma_start(c2[64 * odd:64 * odd + 64, kv, head, 0:SEQ - odd],
                                                  ckv[64 * head:64 * head + 64, kv, odd:SEQ]).then_inc(
                                                      shift_in[kv], 16)

                    def compress():
                        n2 = 2 * NCMP
                        for kv in range(2):
                            for k in range(4 * kv, 4 * kv + 4):
                                act.wait_ge(*done("cmp_part", k))
                                if k + 2 < 8:
                                    load_w1(k + 2)
                            if kv:
                                act.wait_ge(*done("cmp_turned", 0))
                            nc.scalar.activation(hid[0:n2, :], bank_of(("hidden", kv))[0:n2, 0:CMP_HIDDEN],
                                                 ACT.Gelu_apprx_tanh).then_inc(
                                                     *tick("cmp_gelu", kv, frees=("hidden", kv)))
                            if kv == 0:
                                act.wait_ge(*done("kc_raw"))
                                nc.scalar.activation(zs[:, 1, 0:2 * CPAD], kc[:],
                                                     ACT.Square).then_inc(*tick("head_sq", "kc"))
                                head_factor("kc", HEAD, 2 * CPAD)
                        act.wait_ge(*done("cmp_out", 1))
                        act.dma_start(biasA[:], bias_lines(0, NSA_HEADS)).then_inc(bias_in[0], 16)

                    def compressed_scores():
                        act.wait_ge(*done("cmp_minus_max"))
                        nc.scalar.activation(cp[:], cp[:], ACT.Exp).then_inc(*tick("cmp_exp"))
                        for r in range(3):
                            act.wait_ge(*done("cmp_probsT", r))
                            nc.scalar.activation(mixed[0:2 * CPAD, r, :], bank_of(("cmp_turn", r))[0:2 * CPAD, :],
                                                 ACT.Copy).then_inc(*tick("cmp_kept", r, frees=("cmp_turn", r)))

                    def nsa():
                        for n in range(14):
                            if n < 12:
                                for i in range(QT):
                                    act.wait_ge(*done("logits", n, i))
                                    k = 4 * (n % 4) + i
                                    pr = probs[:, n % 2, row0(i):row0(i + 1)]
                                    nc.scalar.activation(pr, pr, ACT.Exp, bias=sm("nm", k), scale=-1.0,
                                                         accum_out=sm("sum", k)).then_inc(*tick("probs", n, i))
                            if 1 <= n <= 12:
                                m = n - 1
                                for j in (0, 2):
                                    act.wait_ge(*done("turned_probs", m, j))
                                    if m >= 2:
                                        act.wait_ge(*done("values_used", m - 2))
                                    nc.scalar.activation(probsT[:, m % 2, col0(j):col0(j + 1)],
                                                         bank_of(("t", m, j))[:, j * P:SEQ],
                                                         ACT.Copy).then_inc(*tick("probsT_a", m, j, frees=("t", m, j)))
                            if n >= 5 and n % 4 == 1:
                                r = (n - 5) // 4
                                act.wait_ge(*done("values_used", 4 * r + 3))
                                nc.scalar.activation(mixed[:, r, :], bank_of(("nsa", r))[:],
                                                     ACT.Copy).then_inc(*tick("mixed", r, frees=("nsa", r)))

                    def diff():
                        for n in range(DIFF_HEADS + 1):
                            if n < DIFF_HEADS:
                                for m in range(2):
                                    for i in range(QT):
                                        act.wait_ge(*done("dlogits", n, m, i))
                                        k = 8 * (n % 2) + 4 * m + i
                                        pr = dp[:, n % 2, m, row0(i):row0(i + 1)]
                                        nc.scalar.activation(pr, pr, ACT.Exp, bias=sm("nm", k), scale=-1.0,
                                                             accum_out=sm("sum", k)).then_inc(
                                                                 *tick("dexp", n, m, i))
                            if n >= 1:
                                d = n - 1
                                for j in (0, 2):
                                    act.wait_ge(*done("dturned_probs", d, j))
                                    if d >= 1:
                                        act.wait_ge(*done("dvalues_used", d - 1))
                                    nc.scalar.activation(dpT[:, col0(j):col0(j + 1)],
                                                         bank_of(("dt", d, j))[:, j * P:SEQ],
                                                         ACT.Copy).then_inc(*tick("dprobsT_a", d, j,
                                                                                  frees=("dt", d, j)))
                        for t in range(2):
                            act.wait_ge(*done("dvalues_used", 2 * t + 1))
                            nc.scalar.activation(zs[:, t, :], bank_of(("diff", t))[:],
                                                 ACT.Square).then_inc(*tick("head_sq", ("diff", t)))
                        for t in range(2):
                            head_factor(("diff", t), HEAD)

                    act.wait_ge(params_in, 32)
                    for k in range(KT):
                        split_x("ffn1", "ffn1", k)
                        square("ffn1", k, x[:, k, :])
                        if k < AHEAD:
                            split(k)
                    ffn("ffn1", "mix", "mix", None)
                    project("C")
                    hgrn()
                    load_compression()
                    project("A")
                    compress()
                    compressed_scores()
                    nsa()
                    act.wait_ge(*done("values_used", 11))
                    act.dma_start(biasB[:], bias_lines(NSA_HEADS, DIFF_HEADS)).then_inc(bias_in[1], 16)
                    project("B")
                    diff()
                    act.wait_ge(*done("product", ("hg2",)))
                    for k in MIX_ORDER:
                        act.wait_ge(*done(*MIXED[k]))
                        nc.scalar.activation(xh[:, k, :], mixed[:, k, :], ACT.Copy).then_inc(*tick("x_hi", "mixed", k))
                    for dt in range(KT):
                        split(CHUNK[("wout", dt)] + AHEAD)
                        act.wait_ge(*done("x_new", "out", dt))
                        square("ffn2", dt, x[:, dt, :])
                    act.wait_ge(*done("product", ("wout", KT - 1)))
                    for dt in range(KT):
                        split_x("ffn2", "ffn2", dt)
                    ffn("ffn2", "ple", "ple", None)
                    act.dma_start(emb[:], a["p"][layer]).then_inc(emb_in, 16)
                    act.wait_ge(emb_in, 16)
                    for k in range(2):
                        nc.scalar.activation(embh[:, k, :], emb[:, k, :], ACT.Copy).then_inc(*tick("emb_hi", k))
                    for dt in range(KT):
                        if dt % 4 == 0:
                            split(CHUNK[("ple_proj", dt // 4)] + AHEAD)
                        key, d = ("ple_proj", dt // 4), dt % 4
                        act.wait_ge(*(done("product", key) if d == 3 else done("product", key, d)))
                        nc.scalar.activation(emby[:, dt, :], bank_of(("ple_out", dt))[:],
                                             ACT.Copy).then_inc(*tick("emb_y", dt, frees=("ple_out", dt)))
                        act.wait_ge(*done("emb_y", dt))
                        square("post", dt, emby[:, dt, :])
                    factor("post", rb2[:])
                    for dt in range(KT):
                        split(CHUNK[("ple_gate", dt)] + AHEAD)
                        if dt == 0:
                            factor("ple", rb[:])
                        act.wait_ge(*done("pgate_scaled", dt))
                        nc.scalar.activation(pg[:, dt % 2, :], pg[:, dt % 2, :],
                                             ACT.Sigmoid).then_inc(*tick("pgate", dt))

                @block.vector
                def _(dve):
                    at = {"lo": 0}

                    def split(upto):
                        while at["lo"] <= min(upto, len(CHUNKS) - 1):
                            c = at["lo"]
                            n = chunk_width(CHUNKS[c])
                            dve.wait_ge(*done("weights_hi", c))
                            nc.vector.tensor_tensor(wl[:, c % SLOTS, 0:n], raw[:, c % SLOTS, 0:n],
                                                    wh[:, c % SLOTS, 0:n], ALU.subtract).then_inc(
                                                        *tick("weights_lo", c))
                            at["lo"] += 1

                    def split_x(stage, gain, k):
                        dve.wait_ge(*done("x_hi", stage, k))
                        nc.vector.scalar_tensor_tensor(out=xl[:, k, :], in0=x[:, k, :], scalar=col(gain, k),
                                                       in1=xh[:, k, :], op0=ALU.mult,
                                                       op1=ALU.subtract).then_inc(*tick("x_lo", stage, k))

                    def add_square(norm, k):
                        if k == 0:
                            return
                        dve.wait_ge(*done("squared", norm, k))
                        if k == 1:
                            if norm != NORMS[0]:
                                dve.wait_ge(*done("squares", NORMS[NORMS.index(norm) - 1]))
                            ins = nc.vector.tensor_tensor(acc[:], sq[:, 0, :], sq[:, 1, :], ALU.add)
                        else:
                            dve.wait_ge(*done("squares_added", norm, k - 1))
                            ins = nc.vector.tensor_tensor(acc[:], acc[:], sq[:, k % 2, :], ALU.add)
                        ins.then_inc(*tick("squares_added", norm, k))

                    def link(ins):
                        at["link"] = at.get("link", 0) + 1
                        ins.then_inc(*tick("link", at["link"]))
                        dve.wait_ge(*done("link", at["link"]))

                    def small_exponents():
                        dve.wait_ge(params_in, 32)
                        V = nc.vector
                        V.tensor_scalar(sm("gq"), col("nq"), HEAD ** -0.5, None, ALU.mult).then_inc(*tick("gains", 0))
                        V.tensor_scalar(sm("gdq"), col("dq"), DIFF_QK ** -0.5, None,
                                        ALU.mult).then_inc(*tick("gains", 1))
                        for b in range(2):
                            V.tensor_scalar(sm("gk", 2 * b, 2), const_("half"), col("nk", 1 + b), None,
                                            ALU.mult).then_inc(*tick("gains", 2 + b))
                        V.tensor_scalar(sm("gdk", 0, 4), const_("quarter"), col("dk"), None,
                                        ALU.mult).then_inc(*tick("gains", 4))
                        V.tensor_scalar(sm("gsub"), col("subln"), col("sub0"), None,
                                        ALU.mult).then_inc(*tick("gains", 5))
                        lam = cols[:, COLS["lam"][0]:COLS["lam"][0] + 128].rearrange("p (a b d) -> p a b d", a=2, b=2)
                        l2 = sm("lam2", 0, 64).rearrange("p (a d) -> p a d", a=2)
                        V.tensor_tensor(sm("max", 0, 3), col("lb", 0, 3), col("lb", 3, 3),
                                        ALU.max).then_inc(*tick("gains", 6))
                        link(V.tensor_tensor(l2, lam[:, :, 0, :], lam[:, :, 1, :], ALU.mult))
                        V.tensor_reduce(sm("e", 6, 2), l2, AX.X, ALU.add).then_inc(*tick("gains", 7))
                        V.tensor_tensor(sm("e", 0, 3), col("lb", 0, 3), sm("max", 0, 3),
                                        ALU.subtract).then_inc(*tick("gains", 8))
                        V.tensor_tensor(sm("e", 3, 3), col("lb", 3, 3), sm("max", 0, 3),
                                        ALU.subtract).then_inc(*tick("exponents"))

                    def small_logarithms():
                        V = nc.vector
                        dve.wait_ge(*done("exponentials"))
                        link(V.tensor_tensor(sm("nlam"), sm("e", 7), sm("e", 6), ALU.subtract))
                        V.tensor_scalar(sm("nlam"), sm("nlam"), col("lam0"), None,
                                        ALU.subtract).then_inc(*tick("gains", 9))
                        link(V.tensor_tensor(sm("tot", 0, 3), sm("e", 0, 3), sm("e", 3, 3), ALU.add))
                        link(V.reciprocal(sm("rec", 0, 3), sm("tot", 0, 3)))
                        link(V.tensor_tensor(sm("e", 0, 3), sm("e", 0, 3), sm("rec", 0, 3), ALU.mult))
                        link(V.tensor_tensor(sm("e", 3, 3), sm("e", 3, 3), sm("rec", 0, 3), ALU.mult))
                        link(V.tensor_tensor(sm("lb", 0, 3), sm("e", 0, 3), sm("e", 3, 3), ALU.add))
                        link(V.tensor_tensor(sm("lb", 0, 3), sm("lb", 0, 3), sm("e", 0, 3), ALU.subtract))
                        link(V.tensor_scalar(sm("lb", 0, 3), sm("lb", 0, 3), col("flag"), None, ALU.mult))
                        link(V.tensor_scalar(sm("lb", 3, 3), sm("lb", 0, 3), -1.0, 1.0, ALU.mult, ALU.add))
                        V.tensor_scalar(sm("li", 0, 6), sm("lb", 0, 6), 0.0, NEG, ALU.is_le,
                                        ALU.mult).then_inc(*tick("gains", 10))
                        V.tensor_scalar(sm("lc", 0, 6), sm("lb", 0, 6), 2.0 ** -60, None,
                                        ALU.max).then_inc(*tick("logarithm_of"))
                        dve.wait_ge(*done("logarithms"))
                        link(V.tensor_tensor(sm("ab", 0, 6), sm("lc", 0, 6), sm("li", 0, 6), ALU.add))

                    def ffn(name, nxt, gain):
                        for ft in range(FT + 2):
                            c = CHUNK[(name + "_gate", min(ft, FT - 1))]
                            if ft < FT:
                                split(c + AHEAD)
                                dve.wait_ge(*done("product", (name + "_gate", ft)))
                                if ft == 0:
                                    dve.wait_ge(*done("factor", name))
                                if ft >= 2:
                                    dve.wait_ge(*done("h", name, ft - 2))
                                nc.vector.tensor_tensor(fg[:, ft % 2, :], bank_of((name + "_gate", ft))[:], rb[:],
                                                        ALU.mult).then_inc(
                                    *tick("gate_scaled", name, ft, frees=(name + "_gate", ft)))
                            if ft >= 2:
                                f = ft - 2
                                dve.wait_ge(*done("h_hi", name, f))
                                nc.vector.tensor_tensor(ffl[:, f, :], fu[:, f % 2, :], ffh[:, f, :],
                                                        ALU.subtract).then_inc(*tick("h_lo", name, f))
                            if ft < FT:
                                split(c + 1 + AHEAD)
                                dve.wait_ge(*done("product", (name + "_up", ft)))
                                if ft >= 2:
                                    dve.wait_ge(*done("h_lo", name, ft - 2))
                                nc.vector.tensor_tensor(fu[:, ft % 2, :], bank_of((name + "_up", ft))[:], rb[:],
                                                        ALU.mult).then_inc(
                                    *tick("up_scaled", name, ft, frees=(name + "_up", ft)))
                                dve.wait_ge(*done("up_scaled", name, ft))
                                dve.wait_ge(*done("gate_silu", name, ft))
                                nc.vector.tensor_tensor(fu[:, ft % 2, :], fu[:, ft % 2, :], fg[:, ft % 2, :],
                                                        ALU.mult).then_inc(*tick("h", name, ft))
                            if name == "ffn1" and ft == 0:
                                small_exponents()
                            if name == "ffn1" and ft == 1:
                                small_logarithms()
                        for dt in range(KT):
                            for third in range(3):
                                split(CHUNK[(name + "_down", dt, third)] + AHEAD)
                            dve.wait_ge(*done("product", (name + "_down", dt, 2)))
                            nc.vector.scalar_tensor_tensor(out=x[:, dt, :], in0=bank_of((name + "_down", dt))[:],
                                                           scalar=0.5, in1=x[:, dt, :], op0=ALU.mult,
                                                           op1=ALU.add).then_inc(
                                *tick("x_new", name, dt, frees=(name + "_down", dt)))
                            dve.wait_ge(*done("x_new", name, dt))
                            split_x(nxt, gain, dt)
                            add_square(nxt, dt)

                    def scaled(name, out):
                        dve.wait_ge(*done("product", (name,)))
                        nc.vector.tensor_tensor(out, bank_of((name,))[:], rb[:],
                                                ALU.mult).then_inc(*tick("scaled", name, frees=(name,)))

                    def normed(name):
                        zz = z[:, TILES.index(name) % 3, :]
                        dve.wait_ge(*done("head_factor", name))
                        dve.wait_ge(*done("scaled", name))
                        t = int(name[-1]) if name[-1].isdigit() else 0
                        if name[:2] == "nq":
                            outs = [(q[:, t, :], sm("gq"))]
                        elif name[:2] == "dq":
                            outs = [(dq[:, t, :], sm("gdq"))]
                        elif name in ("sk", "wk"):
                            b = ("sk", "wk").index(name)
                            outs = [(kpad[:, b, g, :], sm("gk", 2 * b + g)) for g in range(2)]
                        else:
                            outs = [(dkp[:, t, g, :], sm("gdk", g)) for g in range(4)]
                        for n, (out, gain) in enumerate(outs):
                            key = ("normed", name, n - len(outs) + 1)
                            nc.vector.scalar_tensor_tensor(out=out, in0=zz, scalar=gain, in1=rn[:], op0=ALU.mult,
                                                           op1=ALU.mult).then_inc(*tick(*key))

                    def project(group):
                        names = GROUP_OF[group]
                        for j, name in enumerate(names):
                            split(CHUNK[(name,)] + AHEAD)
                            if name == TILES[0]:
                                dve.wait_ge(*done("factor", "mix"))
                            if name[:2] in ("hf", "hq"):
                                scaled(name, {"hf": hf, "hq": hq}[name[:2]][:, int(name[2]), :])
                            elif name in ("ck", "cv"):
                                scaled(name, ckv[:, ("ck", "cv").index(name), :])
                            else:
                                scaled(name, z[:, TILES.index(name) % 3, :])
                            if name == TILES[1]:
                                dve.wait_ge(*done("turned"))
                                nc.vector.tensor_copy(sm("rt", 0, 4), bank_of("turned")[:, 0:SEQ:P]).then_inc(
                                    *tick("factor_turned", frees="turned"))
                            if j and names[j - 1] in NORMED:
                                normed(names[j - 1])
                            if j and names[j - 1][:2] == "hg":
                                gate_out(names[j - 1])
                        if group in NAT:
                            for c in range(4):
                                split(CHUNK[("nat" + group, c)] + AHEAD)
                        if names[-1] in NORMED:
                            normed(names[-1])
                        if names[-1][:2] == "hg":
                            gate_out(names[-1])

                    def gate_out(name):
                        p = int(name[2])
                        dve.wait_ge(*done("out_gate", name))
                        nc.vector.tensor_tensor(mixed[:, 5 + p, :], mixed[:, 5 + p, :],
                                                z[:, TILES.index(name) % 3, :],
                                                ALU.mult).then_inc(*tick("gated", p))

                    def hgrn():
                        V = nc.vector
                        dve.wait_ge(*done("gate_exp"))
                        link(V.tensor_scalar(gates[:], gates[:], 1.0, None, ALU.add))
                        link(V.reciprocal(gates[:], gates[:]))
                        link(V.tensor_scalar(gates[:, 0, 0:18:3], gates[:, 0, 0:18:3], const_("live"), None,
                                             ALU.mult))
                        for p in range(3):
                            f = hf[:, p, :]
                            la, lb = sm("ab", p), sm("ab", 3 + p)
                            dve.wait_ge(*done("forget", p, 2))
                            link(V.scalar_tensor_tensor(out=tb[:], in0=f, scalar=0.0, in1=ta[:], op0=ALU.min,
                                                        op1=ALU.subtract))
                            V.tensor_tensor(f, tb[:], f, ALU.subtract).then_inc(*tick("log_input", p))
                            V.tensor_scalar(tc[:], tb[:], lb, la, ALU.add, ALU.max).then_inc(*tick("log_max", p))
                            V.tensor_scalar(tb[:], tb[:], lb, la, ALU.add,
                                            ALU.subtract).then_inc(*tick("log_gap", p))
                            dve.wait_ge(*done("forget", p, 5))
                            dve.wait_ge(*done("log_max", p))
                            V.tensor_tensor(tc[:], tc[:], tb[:], ALU.add).then_inc(*tick("log_forget", p))
                            dve.wait_ge(*done("forget", p, 6))
                            V.tensor_scalar(f, f, sm("lb", 3 + p), None, ALU.mult).then_inc(*tick("hgrn_k", p))
                            dve.wait_ge(*done("log_forget", p))
                            for t in range(QT):
                                ts = slice(t * P, (t + 1) * P)
                                V.tensor_tensor_scan(cum[:, p, ts], const_("ones"), tc[:, ts], 0.0, ALU.mult,
                                                     ALU.add).then_inc(*tick("cumsum", p, t))
                            dve.wait_ge(*done("cumsum", p, 1))
                            V.tensor_tensor(sm("t01", p), cum[:, p, P - 1:P], cum[:, p, 2 * P - 1:2 * P],
                                            ALU.add).then_inc(*tick("cumsum", p, "t01"))
                        dve.wait_ge(*done("cumsum", 2, "t01"))
                        for p in range(3):
                            def exponents(lev):
                                g = p * LEVELS + lev
                                size = 1 << lev
                                c = cum[:, p, :].rearrange("p (b two l) -> p b two l", two=2, l=size)
                                e = ev[:, g % 2, :].rearrange("p (b two l) -> p b two l", two=2, l=size)
                                ref = c[:, :, 0, size - 1:size].broadcast_to([P, SEQ // (2 * size), size])
                                if g >= 2:
                                    dve.wait_ge(*done("decayed", g - 2, 1))
                                V.tensor_tensor(e[:, :, 0, :], ref, c[:, :, 0, :],
                                                ALU.subtract).then_inc(*tick("exponent", g, 0))
                                V.tensor_tensor(e[:, :, 1, :], c[:, :, 1, :], ref,
                                                ALU.subtract).then_inc(*tick("exponent", g, 1))

                            def keep(lev):
                                for hh in range(2):
                                    out = sdiag[:, hh, :].rearrange("p (t s) -> p t s", t=QT)
                                    key = ("h", p, lev, hh)
                                    src = bank_of(key)[:].rearrange("p (t s) -> p t s", t=QT)
                                    if lev < 0:
                                        dve.wait_ge(*done("hgrn_same", p, hh))
                                        if p:
                                            dve.wait_ge(*done("hgrn_values", p - 1))
                                        eye = const_("ident")[:, None, :].broadcast_to([P, QT, P])
                                        ins = V.tensor_tensor(out, src, eye, ALU.mult)
                                    else:
                                        dve.wait_ge(*done("hgrn_scores", p * LEVELS + lev, hh))
                                        dve.wait_ge(*done("near_scores", p, lev - 1, hh))
                                        m = lmask[:, lev, :].bitcast(U32)[:, None, :].broadcast_to([P, QT, P])
                                        ins = V.copy_predicated(out, m, src)
                                    ins.then_inc(*tick("near_scores", p, lev, hh, frees=key))

                            exponents(0)
                            exponents(1)
                            for lev in range(-1, 7):
                                keep(lev)
                                if 2 <= lev + 2 < 7 and lev >= 0:
                                    exponents(lev + 2)
                            out_norm(("hgrn", p), 5 + p, col("hout"), "hgrn_out", p)

                    def out_norm(key, tile, gain, kind, n):
                        dve.wait_ge(*done("head_factor", key))
                        nc.vector.scalar_tensor_tensor(out=mixed[:, tile, :], in0=bank_of(key)[:], scalar=gain,
                                                       in1=rn[:], op0=ALU.mult, op1=ALU.mult).then_inc(
                                                           *tick(kind, n, frees=key))

                    def compress():
                        V = nc.vector
                        n2 = 2 * NCMP
                        dve.wait_ge(w2_in, 16)
                        dve.wait_ge(*done("zeros", "vc"))
                        for kv in range(2):
                            V.tensor_copy(w2p[:, kv, :, 1, :], w2s[:, kv]).then_inc(*tick("w2_padded", kv))
                        for kv in range(2):
                            dve.wait_ge(shift_in[kv], 64)
                            if kv:
                                dve.wait_ge(*done("cmp_part", 3))
                            src = bass.AP(c2, kv * 2 * SEQ, [[4 * SEQ, P], [2, PAIRS], [SEQ, 2], [CMP_STRIDE, NCMP]])
                            pos = cols[:, COLS["pos"][0] + kv * PAIRS:COLS["pos"][0] + (kv + 1) * PAIRS]
                            pos = pos[:, :, None].broadcast_to([P, PAIRS, n2])
                            V.tensor_tensor(w2c[:].rearrange("p m (h n) -> p m h n", h=2), src,
                                            pos.rearrange("p m (h n) -> p m h n", h=2),
                                            ALU.add).then_inc(*tick("windows", kv))
                            dve.wait_ge(*done("cmp_turned", kv))
                            if kv:
                                dve.wait_ge(*done("cmp_made", 0))
                            V.tensor_copy(hidT[:].rearrange("p k n -> p (k n)"),
                                          bank_of(("hiddenT", kv))[:, 0:2 * n2]).then_inc(
                                              *tick("hidT", kv, frees=("hiddenT", kv)))
                            dve.wait_ge(*done("cmp_made", kv))
                            o = bank_of(("compressed", kv))
                            if kv == 0:
                                kv3 = kc[:].rearrange("p (g n) -> p g n", g=2)[:, :, 0:NCMP]
                                V.tensor_copy(kv3, o[:, 0:2 * CPAD].rearrange("p (g n) -> p g n", g=2)[:, :, 0:NCMP]
                                              ).then_inc(*tick("kc_raw", frees=("compressed", 0)))
                                dve.wait_ge(*done("kc_raw"))
                                dve.wait_ge(*done("head_factor", "kc"))
                                V.scalar_tensor_tensor(out=kc[:], in0=kc[:], scalar=col("nk", 0),
                                                       in1=rn[:, 0:2 * CPAD], op0=ALU.mult,
                                                       op1=ALU.mult).then_inc(*tick("kc"))
                            else:
                                for g in range(2):
                                    rows = slice(CPAD * g, CPAD * g + NCMP)
                                    V.tensor_copy(vc[rows, :], o[rows, 0:P]).then_inc(
                                        *(tick("vc", g, frees=("compressed", 1)) if g else tick("vc", g)))
                        dve.wait_ge(*done("vc", 1))
                        V.memset(sm("cmax"), 0.0).then_inc(*tick("cmp_out", 1))

                    def compressed_scores():
                        V = nc.vector
                        mask = const_("cmask")
                        for part, (r0, nr) in enumerate(((0, 2), (2, 1))):
                            dve.wait_ge(*done("cmp_scores", part))
                            w = QT * 2 * CPAD
                            V.tensor_tensor(cp[:, r0 * QT:(r0 + nr) * QT, :].rearrange("p (r i) n -> p r (i n)", r=nr),
                                            bank_of(("cmp_scores", part))[:, 0:nr * w].rearrange(
                                                "p (r n) -> p r n", r=nr),
                                            mask[:, None, :].broadcast_to([P, nr, w]), ALU.add).then_inc(
                                                *tick("cmp_masked", part, frees=("cmp_scores", part)))
                        flat = cp[:].rearrange("p a (g n) -> p (a g) n", g=2)
                        dve.wait_ge(*done("cmp_masked", 1))
                        link(V.tensor_reduce(sm("cmax", 0, 24), flat, AX.X, ALU.max))
                        V.tensor_tensor(flat, flat, sm("cmax", 0, 24)[:, :, None].broadcast_to([P, 24, CPAD]),
                                        ALU.subtract).then_inc(*tick("cmp_minus_max"))
                        dve.wait_ge(*done("cmp_exp"))
                        link(V.tensor_reduce(sm("csum", 0, 24), flat, AX.X, ALU.add))
                        link(V.reciprocal(sm("csum", 0, 24), sm("csum", 0, 24)))
                        for r in range(3):
                            gate = gates[:, :, 3 * r:3 * r + 10:9]
                            V.tensor_tensor(sm("ccoef", 8 * r, 8).rearrange("p (i g) -> p i g", g=2),
                                            sm("csum", 8 * r, 8).rearrange("p (i g) -> p i g", g=2), gate,
                                            ALU.mult).then_inc(*tick("ccoef", r))
                        dve.wait_ge(*done("ccoef", 2))
                        V.tensor_tensor(flat, flat, sm("ccoef", 0, 24)[:, :, None].broadcast_to([P, 24, CPAD]),
                                        ALU.mult).then_inc(*tick("cmp_probs"))

                    def logits(out, content, bias, k, name, key, n):
                        nc.vector.tensor_tensor_reduce(out=out, in0=bank_of(content)[:, 0:n], in1=bias, scale=-1.0,
                                                       scalar=3e38, op0=ALU.add, op1=ALU.min,
                                                       accum_out=sm("nm", k)).then_inc(
                                                           *tick(name, *key, frees=content))

                    def nsa():
                        V = nc.vector
                        dve.wait_ge(bias_in[0], 16)
                        for n in range(14):
                            if n >= 2:
                                for j in (1, 3):
                                    evacuate(n - 2, j)
                            if n < 12:
                                r, g = n // 4, n // 2 % 2
                                for i in range(QT):
                                    dve.wait_ge(*done("scores", n, i))
                                    if n >= 2:
                                        dve.wait_ge(*done("turned_probs", n - 2, QT - 1))
                                    logits(probs[:, n % 2, row0(i):row0(i + 1)], ("s", n, i),
                                           biasA[:, g * GROUP + r, SEQ - (i + 1) * P:SEQ], 4 * (n % 4) + i, "logits",
                                           (n, i), (i + 1) * P)
                            if 1 <= n <= 12:
                                scale(n - 1)

                    def evacuate(m, j):
                        dve.wait_ge(*done("turned_probs", m, j))
                        if m >= 2:
                            dve.wait_ge(*done("values_used", m - 2))
                        nc.vector.tensor_copy(probsT[:, m % 2, col0(j):col0(j + 1)],
                                              bank_of(("t", m, j))[:, j * P:SEQ]).then_inc(
                                                  *tick("probsT_v", m, j, frees=("t", m, j)))

                    def scale(m):
                        V = nc.vector
                        r, g, b = m // 4, m // 2 % 2, m % 2
                        k = 4 * (m % 4)
                        dve.wait_ge(*done("probs", m, QT - 1))
                        link(V.reciprocal(sm("coef", k, 4), sm("sum", k, 4)))
                        link(V.tensor_tensor(sm("coef", k, 4), sm("coef", k, 4),
                                             gates[:, :, (g * GROUP + r) * 3 + 1 + b], ALU.mult))
                        for i in range(QT):
                            pr = probs[:, m % 2, row0(i):row0(i + 1)]
                            V.tensor_scalar(pr, pr, sm("coef", k + i), None,
                                            ALU.mult).then_inc(*tick("probs_scaled", m, i))

                    def diff():
                        V = nc.vector
                        dve.wait_ge(bias_in[1], 16)
                        for n in range(DIFF_HEADS + 2):
                            if n >= 2:
                                for j in (1, 3):
                                    devacuate(n - 2, j)
                            if n < DIFF_HEADS:
                                for m in range(2):
                                    for i in range(QT):
                                        dve.wait_ge(*done("dscores", n, m, i))
                                        if n >= 2:
                                            dve.wait_ge(*done("dturned_probs", n - 2, QT - 1))
                                        logits(dp[:, n % 2, m, row0(i):row0(i + 1)], ("ds", n, m, i),
                                               biasB[:, n, SEQ - (i + 1) * P:SEQ], 8 * (n % 2) + 4 * m + i,
                                               "dlogits", (n, m, i), (i + 1) * P)
                            if 1 <= n <= DIFF_HEADS:
                                d = n - 1
                                k = 8 * (d % 2)
                                dve.wait_ge(*done("dexp", d, 1, QT - 1))
                                link(V.reciprocal(sm("coef", k, 8), sm("sum", k, 8)))
                                link(V.tensor_scalar(sm("coef", k + 4, 4), sm("coef", k + 4, 4), sm("nlam"), None,
                                                     ALU.mult))
                                for i in range(QT):
                                    second = dp[:, d % 2, 1, row0(i):row0(i + 1)]
                                    V.tensor_scalar(second, second, sm("coef", k + 4 + i), None,
                                                    ALU.mult).then_inc(*tick("dsecond", d, i))
                                for i in range(QT):
                                    first = dp[:, d % 2, 0, row0(i):row0(i + 1)]
                                    second = dp[:, d % 2, 1, row0(i):row0(i + 1)]
                                    dve.wait_ge(*done("dsecond", d, i))
                                    V.scalar_tensor_tensor(out=first, in0=first, scalar=sm("coef", k + i), in1=second,
                                                           op0=ALU.mult, op1=ALU.add).then_inc(
                                                               *tick("dprobs", d, i))
                        for t in range(2):
                            out_norm(("diff", t), 3 + t, sm("gsub"), "diff_out", t)

                    def devacuate(d, j):
                        dve.wait_ge(*done("dturned_probs", d, j))
                        if d >= 1:
                            dve.wait_ge(*done("dvalues_used", d - 1))
                        nc.vector.tensor_copy(dpT[:, col0(j):col0(j + 1)],
                                              bank_of(("dt", d, j))[:, j * P:SEQ]).then_inc(
                                                  *tick("dprobsT_v", d, j, frees=("dt", d, j)))

                    for k in range(KT):
                        if k < AHEAD:
                            split(k)
                        split_x("ffn1", "ffn1", k)
                        add_square("ffn1", k)
                    ffn("ffn1", "mix", "mix")
                    project("C")
                    hgrn()
                    project("A")
                    compress()
                    compressed_scores()
                    nsa()
                    project("B")
                    diff()
                    for k in MIX_ORDER:
                        dve.wait_ge(*done("x_hi", "mixed", k))
                        nc.vector.tensor_tensor(xl[:, k, :], mixed[:, k, :], xh[:, k, :],
                                                ALU.subtract).then_inc(*tick("x_lo", "mixed", k))
                    for dt in range(KT):
                        split(CHUNK[("wout", dt)] + AHEAD)
                        dve.wait_ge(*done("product", ("wout", dt)))
                        nc.vector.tensor_tensor(x[:, dt, :], bank_of(("wout", dt))[:], x[:, dt, :],
                                                ALU.add).then_inc(*tick("x_new", "out", dt, frees=("wout", dt)))
                        add_square("ffn2", dt)
                    for dt in range(KT):
                        dve.wait_ge(*done("x_new", "out", dt))
                        split_x("ffn2", "ffn2", dt)
                    ffn("ffn2", "ple", "ple")
                    for k in range(2):
                        dve.wait_ge(*done("emb_hi", k))
                        nc.vector.tensor_tensor(embl[:, k, :], emb[:, k, :], embh[:, k, :],
                                                ALU.subtract).then_inc(*tick("emb_lo", k))
                    for dt in range(KT):
                        if dt % 4 == 0:
                            split(CHUNK[("ple_proj", dt // 4)] + AHEAD)
                        add_square("post", dt)
                    dve.wait_ge(*done("factor", "post"))
                    for dt in range(KT):
                        nc.vector.scalar_tensor_tensor(out=emby[:, dt, :], in0=emby[:, dt, :], scalar=col("post", dt),
                                                       in1=rb2[:], op0=ALU.mult,
                                                       op1=ALU.mult).then_inc(*tick("emb_normed", dt))
                    for dt in range(KT):
                        split(CHUNK[("ple_gate", dt)] + AHEAD)
                        dve.wait_ge(*done("product", ("ple_gate", dt)))
                        if dt == 0:
                            dve.wait_ge(*done("factor", "ple"))
                        nc.vector.tensor_tensor(pg[:, dt % 2, :], bank_of(("ple_gate", dt))[:], rb[:],
                                                ALU.mult).then_inc(*tick("pgate_scaled", dt, frees=("ple_gate", dt)))
                        dve.wait_ge(*done("pgate", dt))
                        dve.wait_ge(*done("emb_normed", dt))
                        nc.vector.tensor_tensor(pg[:, dt % 2, :], pg[:, dt % 2, :], emby[:, dt, :],
                                                ALU.mult).then_inc(*tick("pgated", dt))
                        dve.wait_ge(*done("pgated", dt))
                        nc.vector.tensor_tensor(x[:, dt, :], x[:, dt, :], pg[:, dt % 2, :],
                                                ALU.add).then_inc(*tick("x_new", "ple", dt))

            with nc.Block() as block:
                @block.sync
                def _(sp):
                    nums = [s.num for s in (*cleared, *counts.sems.values())]
                    assert len(nums) == max(nums) - min(nums) + 1
                    sp.sem_clear(range(min(nums), max(nums) + 1))

        with nc.Block() as block:
            @block.sync
            def _(sp):
                sp.dma_start(a["out"], x[:]).then_inc(x_out, 16)
                sp.wait_ge(x_out, 16)
        return counts.facts()


NORMS = ["ffn1", "mix", "ffn2", "ple", "post"]
MIXED = {**{r: ("mixed", r) for r in range(3)}, **{3 + t: ("diff_out", t) for t in range(2)},
         **{5 + p: ("gated", p) for p in range(3)}}
MIX_ORDER = list(range(KT))
_order = [("hgrn", p) for p in range(3)] + NORMED[0:5] + ["kc"] + NORMED[5:9] + [("diff", t) for t in range(2)]
_reader = {**{("hgrn", p): ("hgrn_out", p) for p in range(3)}, **{n: ("normed", n, 0) for n in NORMED}, "kc": ("kc",),
           **{("diff", t): ("diff_out", t) for t in range(2)}}
RN_BEFORE = {name: (_reader[_order[n - 1]] if n else None) for n, name in enumerate(_order)}


def bucket_of(distance):
    n = np.maximum(distance, 0)
    exact = BUCKETS // 2
    nf = np.maximum(n, 1).astype(np.float32)
    far = exact + (np.log(nf / exact) / math.log(MAX_DISTANCE / exact) * (BUCKETS - exact)).astype(np.int32)
    return np.where(n < exact, n, np.minimum(far, BUCKETS - 1))


def shape_constants():
    c = np.zeros((P, NCONST), np.float32)

    def put(name, value):
        at, n = CONST[name]
        c[:, at:at + n] = value

    p = np.arange(P)
    put("ident", np.eye(P))
    put("ones", 1.0)
    put("sum64", p[:, None] // 64 == p[None] // 64)
    put("sum32", p[:, None] // 32 == p[None] // 32)
    put("half", p[:, None] // 64 == np.arange(2))
    put("quarter", p[:, None] // 32 == np.arange(4))
    n = np.arange(CPAD)
    t = np.arange(QT)[None, :, None, None] * P + p[:, None, None, None]
    ok = (n < NCMP) & (CMP_STRIDE * n + CMP_BLOCK - 1 <= t)
    put("cmask", np.where(np.broadcast_to(ok, (P, QT, 2, CPAD)), 0.0, NEG).reshape(P, -1))
    put("live", (p >= CMP_BLOCK - 1)[:, None])
    put("eps", EPS)
    put("one", 1.0)
    distance = SEQ - 1 - np.arange(LINE)
    row = np.where(distance < 0, BUCKETS, bucket_of(distance))
    onehot = (np.arange(BUCKETS + 1)[:, None] == row[None]).astype(np.float32)
    s, t = p[:, None], p[None, :]
    masks = np.zeros((P, 7, P), np.float32)
    for lev in range(7):
        size = 1 << lev
        masks[:, lev] = (s // (2 * size) == t // (2 * size)) & (s // size % 2 == 0) & (t // size % 2 == 1)
    return c, onehot, masks


def lay_out(i):
    D = DEPTH
    out = {}
    out["x"] = i["x"][0].T.reshape(KT, P, SEQ).transpose(1, 0, 2)
    out["p"] = i["p"][:, 0].transpose(0, 2, 1).reshape(D, 2, P, SEQ).transpose(0, 2, 1, 3)
    out["rel_bias"] = i["rel_bias"]
    for name in ("ffn1", "ffn2"):
        for part in ("gate", "up"):
            w = i[f"{name}_w_{part}"].reshape(D, KT, P, FT, P)
            out[f"{name}_{part}"] = w.transpose(0, 3, 2, 1, 4).reshape(D, FT, P, WIDE)
        w = i[f"{name}_w_down"].reshape(D, FT, P, KT, P)
        out[f"{name}_down"] = w.transpose(0, 3, 2, 1, 4).reshape(D, KT, P, FT * P)
    w = i["w_in"]
    widths = (384, 128, 128, 128, 128, 128, 128, 18, 256, 256, 256, 384, 384, 384, 384)
    names = ("nq", "ck", "cv", "sk", "sv", "wk", "wv", "ng", "dq", "dk", "dv", "hq", "hf", "hi", "hg")
    cut = dict(zip(names, np.split(w, np.cumsum(widths)[:-1].tolist(), axis=2)))
    nq = cut["nq"].reshape(D, D_MODEL, NSA_KV, GROUP, HEAD).transpose(0, 1, 3, 2, 4).reshape(D, D_MODEL, 384)
    parts = {**cut, "nq": nq}
    tiles = []
    for name in TILES:
        t = int(name[2]) if len(name) == 3 else 0
        tiles.append(parts[name[:2]][:, :, t * P:(t + 1) * P])
    w = np.stack(tiles, 1).reshape(D, len(TILES), KT, P, P)
    out["w_in_t"] = w.transpose(0, 1, 3, 2, 4).reshape(D, len(TILES), P, WIDE)
    for group, list_ in (("C", ("hi", "ng")), ("A", ("sv", "wv", "dv"))):
        w = np.concatenate([cut[n] for n in list_], 2).reshape(D, 4, 2, P, NAT[group])
        out["nat" + group] = w.transpose(0, 1, 3, 2, 4).reshape(D, 4, P, 2 * NAT[group])
    w = i["w_out"]
    nsa = w[:, 0:384].reshape(D, NSA_KV, GROUP, HEAD, D_MODEL).transpose(0, 2, 1, 3, 4).reshape(D, 384, D_MODEL)
    w = np.concatenate([nsa, w[:, 384:]], 1).reshape(D, KT, P, KT, P)
    out["wout"] = w.transpose(0, 3, 2, 1, 4).reshape(D, KT, P, WIDE)
    w = i["ple_w_gate"].reshape(D, KT, P, KT, P)
    out["ple_gate"] = w.transpose(0, 3, 2, 1, 4).reshape(D, KT, P, WIDE)
    w = i["ple_w_proj"].reshape(D, 2, P, 2, 4, P)
    out["ple_proj"] = w.transpose(0, 3, 2, 4, 1, 5).reshape(D, 2, P, WIDE)
    w = i["nsa_cmp_w1"].reshape(D, 2, 4, 4, P, CMP_HIDDEN)
    out["cmp_w1"] = w.transpose(0, 1, 2, 4, 3, 5)
    out["cmp_w2"] = i["nsa_cmp_w2"].reshape(D, 2, 2, P, HEAD).transpose(0, 3, 1, 2, 4)

    def tiled(v, n):
        return np.tile(v, (1, n))[:, :, None]

    by_tile = [i[n].reshape(D, KT, P).transpose(0, 2, 1)
               for n in ("ffn1_norm", "mix_norm", "ffn2_norm", "ple_norm", "ple_post_norm")]
    k_norm = np.concatenate([tiled(i["nsa_k_norm"][:, b], 2) for b in range(3)], 2)
    lb = np.broadcast_to(i["hgrn_lb_logits"].reshape(1, DEPTH * 3, P), (D, DEPTH * 3, P)).transpose(0, 2, 1)
    lam = np.broadcast_to(i["diff_lambda"].reshape(D, 1, 128), (D, P, 128))
    pos = i["nsa_cmp_pos"].reshape(D, 2, PAIRS, P).transpose(0, 3, 1, 2).reshape(D, P, 2 * PAIRS)
    out["params"] = np.concatenate(
        [*by_tile, tiled(i["nsa_q_norm"], 2), k_norm, tiled(i["diff_q_norm"], 4), tiled(i["diff_k_norm"], 4),
         tiled(i["diff_subln"], 2), tiled(i["hgrn_out_norm"], 2), lb, lam, pos], 2)
    lam0 = [0.8 - 0.6 * math.exp(-0.3 * layer) for layer in range(D)]
    rows = np.array([[float(layer > 0), lam0[layer], 1.0 - lam0[layer]] for layer in range(D)], np.float32)
    out["layer_consts"] = np.broadcast_to(rows[:, None, :], (D, P, 3))
    out["consts"], out["onehot"], out["level_masks"] = shape_constants()
    return {k: np.ascontiguousarray(v) for k, v in out.items()}


def program(nc, arrays, known):
    a = {name: nc.dram_tensor(f"in_{name}", v.shape, mybir.dt.from_np(v.dtype), kind="ExternalInput").ap()
         for name, v in arrays.items()}
    a["out"] = nc.dram_tensor("out_0", (P, KT, SEQ), F32, kind="ExternalOutput").ap()
    return layers(nc, a, known)


def kernel(**inputs):
    import concourse.bacc as bacc
    from concourse.bass_utils import run_bass_kernel_spmd

    arrays = lay_out({k: np.asarray(v) for k, v in inputs.items()})
    known = program(bacc.Bacc("TRN2", target_bir_lowering=False, num_devices=1), arrays, {})
    nc = bacc.Bacc("TRN2", target_bir_lowering=False, num_devices=1)
    program(nc, arrays, known)
    r = run_bass_kernel_spmd(nc, [{f"in_{k}": v for k, v in arrays.items()}], core_ids=[0])
    out = r.results[0]["out_0"]
    return out.transpose(1, 0, 2).reshape(D_MODEL, SEQ).T.reshape(1, SEQ, D_MODEL)
```

```python
import math
from contextlib import ExitStack

import numpy as np

import concourse.bass as bass
from concourse import mybir
from concourse.alu_op_type import AluOpType as ALU

ACT = mybir.ActivationFunctionType
AX = mybir.AxisListType
F32 = mybir.dt.float32
F32R = mybir.dt.float32r
U32 = mybir.dt.uint32

P = 128
D_MODEL, SEQ, DEPTH, PLE_DIM, D_FF = 1024, 512, 2, 256, 2816
HEAD = 64
BUCKETS, MAX_DISTANCE = 32, 128
NEG = -1e30
EPS = 1e-6
NSA_HEADS, NSA_KV, GROUP = 6, 2, 3
CMP_BLOCK, CMP_STRIDE, CMP_HIDDEN = 32, 16, 256
NCMP = SEQ // CMP_STRIDE - 1
CPAD = 32
PAIRS = CMP_BLOCK // 2
DIFF_HEADS, DIFF_QK = 4, 32
HGRN_HEADS = 6
KT = D_MODEL // P
FT = D_FF // P
QT = SEQ // P
THIRDS = ((0, 8), (8, 15), (15, 22))
BIAS_HEADS = NSA_HEADS + DIFF_HEADS
LINE = P + SEQ
WIDE = KT * P
SLOTS = 3
LINES_IN_AT, LINES_OUT_AT = 10, 12
AHEAD = 2
LEVELS = 9

_at = 0
COLS = {}
for _name, _n in (("ffn1", 8), ("mix", 8), ("ffn2", 8), ("ple", 8), ("post", 8), ("nq", 1), ("nk", 3), ("dq", 1),
                  ("dk", 1), ("subln", 1), ("hout", 1), ("lb", 6), ("lam", 128), ("pos", 32), ("flag", 1),
                  ("lam0", 1), ("sub0", 1)):
    COLS[_name] = (_at, _n)
    _at += _n
NCOLS = _at
NPARAM = COLS["flag"][0]

_at = 0
CONST = {}
for _name, _n in (("ident", 128), ("ones", 128), ("sum64", 128), ("sum32", 128), ("half", 2), ("quarter", 4),
                  ("cmask", QT * 2 * CPAD), ("live", 1), ("eps", 1), ("one", 1)):
    CONST[_name] = (_at, _n)
    _at += _n
NCONST = _at

_at = 0
SMALL = {}
for _name, _n in (("gq", 1), ("gdq", 1), ("gk", 4), ("gdk", 4), ("gsub", 1), ("nlam", 1), ("lam2", 64), ("e", 8),
                  ("max", 3), ("tot", 3), ("rec", 3), ("lb", 6), ("lc", 6), ("li", 6), ("ab", 6), ("rt", 4),
                  ("nm", 16), ("sum", 16), ("coef", 16), ("t01", 3), ("cmax", 24), ("csum", 24), ("ccoef", 24)):
    SMALL[_name] = (_at, _n)
    _at += _n
NSMALL = _at

TILES = ["ck", "cv", "hf0", "hf1", "hf2", "hq0", "hq1", "hq2", "sk", "wk", "nq0", "nq1", "nq2", "dk0", "dk1", "dq0",
         "dq1", "hg0", "hg1", "hg2"]
NORMED = ["sk", "wk", "nq0", "nq1", "nq2", "dk0", "dk1", "dq0", "dq1"]
Z_SLOT = {name: n % 3 for n, name in enumerate(TILES[8:])}
GROUP_OF = {"C": TILES[0:8], "A": TILES[8:13], "B": TILES[13:20]}
NAT = {"C": 402, "A": 512}
STEPS = {"C": 12, "A": 9}
BESIDE_HGRN = {(0, 1): 0, (0, 4): 1, (0, 8): 2, (1, 1): 3, (1, 5): 4, (2, 0): 5, (2, 2): 6, (2, 5): 7, (2, 8): 8}
BESIDE_NSA = {0: 0, 2: 1, 5: 2, 6: 3, 9: 4, 10: 5, 11: 6}
W1_SLOTS = 3
CMP_PART_AT = {0: 2, 1: 3, 2: 3, 3: 4, 4: 5, 5: 6, 6: 7, 7: 8}


def chunk_order():
    order = []
    for name in ("ffn1", "mix", "ffn2"):
        if name == "mix":
            for group in "CAB":
                order += [(tile,) for tile in GROUP_OF[group]]
                if group in NAT:
                    order += [("nat" + group, c) for c in range(4)]
            order += [("wout", dt) for dt in range(KT)]
            continue
        for ft in range(FT):
            order += [(name + "_gate", ft), (name + "_up", ft)]
        for dt in range(KT):
            order += [(name + "_down", dt, third) for third in range(3)]
    order += [("ple_proj", h) for h in range(2)]
    order += [("ple_gate", dt) for dt in range(KT)]
    return order


CHUNKS = chunk_order()
CHUNK = {key: n for n, key in enumerate(CHUNKS)}


def chunk_width(key):
    if key[0].startswith("nat"):
        return 2 * NAT[key[0][3]]
    if key[0].endswith("_down"):
        a, b = THIRDS[key[2]]
        return (b - a) * P
    return WIDE


def row0(i):
    return P * i * (i + 1) // 2


def col0(j):
    return P * (QT * j - j * (j - 1) // 2)


SCORES = row0(QT)


class Counts:

    def __init__(self, nc, ctx, known):
        self.nc, self.ctx, self.known = nc, ctx, known
        self.sems, self.n, self.seen, self.bank, self.frees, self.slot = {}, {}, {}, {}, {}, {}
        for kind in known.get("kinds", ()):
            self.sem(kind)

    def sem(self, kind):
        if kind not in self.sems:
            self.sems[kind] = self.ctx.enter_context(self.nc.semaphore(kind))
        return self.sems[kind]

    def tick(self, kind, *key, frees=None):
        self.n[kind] = self.n.get(kind, 0) + 1
        assert (kind, *key) not in self.seen, (kind, *key)
        self.seen[(kind, *key)] = self.n[kind]
        if frees is not None:
            assert frees not in self.frees, frees
            self.frees[frees] = (kind, *key)
        return self.sem(kind), 1

    def done(self, kind, *key):
        if not self.known:
            return self.sem(kind), 1
        return self.sem(kind), self.known["seen"][(kind, *key)]

    def freed(self, content):
        if not self.known:
            return self.sem("any"), 1
        return self.done(*self.known["frees"][content])

    def facts(self):
        return {"kinds": sorted(k for k in self.sems if k != "any"), "seen": self.seen, "frees": self.frees,
                "bank": self.bank, "slot": self.slot}


def layers(nc, a, known):
    nc.disable_value_cache = True
    ctx = ExitStack()
    with ctx:
        def sem(name):
            return ctx.enter_context(nc.semaphore(name))

        place = {"at": 16512}

        def sb(name, shape, dt=F32):
            size = int(np.prod(shape[1:])) * 4
            t = nc.alloc_sbuf_tensor_at(name, shape, dt, offset=place["at"])
            place["at"] += (size + 31) // 32 * 32
            assert place["at"] <= 229344, (name, place["at"])
            return t

        x = sb("x_res", [P, KT, SEQ])
        xh, xl = sb("xh", [P, KT, SEQ], F32R), sb("xl", [P, KT, SEQ], F32R)
        raw = sb("raw", [P, SLOTS, WIDE])
        wh, wl = sb("wh", [P, SLOTS, WIDE], F32R), sb("wl", [P, SLOTS, WIDE], F32R)
        const = sb("const", [P, NCONST])
        lmask = sb("lmask", [P, 7, P])
        cols = sb("cols", [P, NCOLS])
        small = sb("small", [P, NSMALL])
        rb, acc = sb("rb", [P, SEQ]), sb("acc", [P, SEQ])
        sq = sb("sq", [P, 2, SEQ])
        region = place["at"]
        ffh, ffl = sb("ffh", [P, FT, SEQ], F32R), sb("ffl", [P, FT, SEQ], F32R)
        fg, fu = sb("fg", [P, 2, SEQ]), sb("fu", [P, 2, SEQ])
        place["at"] = region
        emb = sb("emb", [P, 2, SEQ])
        embh, embl = sb("embh", [P, 2, SEQ], F32R), sb("embl", [P, 2, SEQ], F32R)
        emby = sb("emby", [P, KT, SEQ])
        rb2 = sb("rb2", [P, SEQ])
        pg = sb("pg", [P, 2, SEQ])
        place["at"] = region
        mixed = sb("mixed", [P, KT, SEQ])
        gates = sb("gates", [P, QT, 18])
        z = sb("z", [P, 3, SEQ])
        zs, rn = sq, [sb("rn", [P, SEQ]), acc]
        kc, vc = sb("kc", [P, 2 * CPAD]), sb("vc", [P, P])
        group_a = place["at"]
        q = sb("q", [P, 3, SEQ])
        kpad = sb("kpad", [P, 2, NSA_KV, SEQ])
        vpad = sb("vpad", [P, 2, QT, 4, HEAD])
        dv = sb("dv", [P, QT, 2, 4, HEAD])
        rest = place["at"]
        place["at"] = group_a
        c2 = sb("c2", [P, 2, 2, SEQ])
        w2c = sb("w2c", [P, PAIRS, 2 * NCMP])
        w1 = sb("w1", [P, W1_SLOTS, 4, CMP_HIDDEN])
        w2s = sb("w2s", [P, 2, 2, HEAD])
        w2p = sb("w2p", [P, 2, 2, 3, HEAD])
        hid = sb("hid", [P, CMP_HIDDEN])
        hidT = sb("hidT", [P, 2, 2 * NCMP])
        assert place["at"] <= rest
        place["at"] = rest
        ckv = sb("ckv", [P, 2, SEQ])
        place["at"] = rest
        cp = sb("cp", [P, 12, 2 * CPAD])
        place["at"] = rest
        dq = sb("dqt", [P, 2, SEQ])
        hgrn0 = place["at"]
        hf, hq = sb("hf", [P, 3, SEQ]), sb("hq", [P, 3, SEQ])
        cum = sb("cum", [P, 3, SEQ])
        ev, zv = sb("ev", [P, 2, SEQ]), sb("zv", [P, 2, SEQ])
        sdiag = sb("sdiag", [P, 2, SEQ])
        gate0 = place["at"]
        soff = sb("soff", [P, 2, 6 * P])
        hv = sb("hv", [P, QT, 3, 4, HEAD])
        hgrn_end = place["at"]
        place["at"] = gate0
        ta, tb, tc = sb("ta", [P, SEQ]), sb("tb", [P, SEQ]), sb("tc", [P, SEQ])
        place["at"] = hgrn0
        biasA = sb("biasA", [P, NSA_HEADS, SEQ])
        probs = sb("probs", [P, 2, SCORES])
        probsT = sb("probsT", [P, 2, SCORES])
        place["at"] = hgrn_end - 4 * 2 * 4 * SEQ
        dkp = sb("dkp", [P, 2, 4, SEQ])
        place["at"] = hgrn0
        dp = sb("dp", [P, 2, 2, SCORES])
        place["at"] = hgrn0 + 4 * (NSA_HEADS * SEQ + 2 * SCORES)
        dpT = sb("dpT", [P, SCORES])
        place["at"] = group_a + 4 * 3 * SEQ
        biasB = sb("biasB", [P, DIFF_HEADS, SEQ])
        place["at"] = 229344 - 4 * (2 * LINE + 16)
        tab = sb("tab", [P, BIAS_HEADS])
        onehot = sb("onehot_sb", [P, LINE])
        line = sb("line", [P, LINE])

        main = [ctx.enter_context(nc.psum_tensor(f"main{b}", [P, SEQ], F32)) for b in range(4)]
        side = [ctx.enter_context(nc.psum_tensor(f"side{b}", [P, SEQ], F32)) for b in range(4)]
        line_once = nc.dram_tensor("bias_line", [BIAS_HEADS, LINE], F32).ap()
        lines = nc.dram_tensor("bias_lines", [BIAS_HEADS, P, LINE], F32).ap()

        def const_(name):
            at, n = CONST[name]
            return const[:, at:at + n]

        def col(name, k=0, n=1):
            at = COLS[name][0] + k
            return cols[:, at:at + n]

        def sm(name, k=0, n=1):
            at = SMALL[name][0] + k
            return small[:, at:at + n]

        const_in, x_in, tab_ready, line_made, line_read, line_kept, x_out = (
            sem(n) for n in ("const_in", "x_in", "tab_ready", "line_made", "line_read", "line_kept", "x_out"))
        with nc.Block() as block:
            @block.sync
            def _(sp):
                sp.dma_start(const[:], a["consts"]).then_inc(const_in, 16)
                sp.dma_start(lmask[:], a["level_masks"]).then_inc(const_in, 16)
                sp.dma_start(onehot[0:33, :], a["onehot"]).then_inc(const_in, 16)
                sp.dma_start(tab[0:BUCKETS, :], a["rel_bias"]).then_inc(const_in, 16)
                sp.dma_start(x[:], a["x"]).then_inc(x_in, 16)
                sp.wait_ge(line_read, 2)
                sp.dma_start(line_once, line[0:BIAS_HEADS, :]).then_inc(line_kept, 16)
                sp.wait_ge(line_kept, 16)

            @block.gpsimd
            def _(pool):
                nc.gpsimd.memset(tab[BUCKETS:BUCKETS + 1, :], NEG).then_inc(tab_ready, 1)

            @block.tensor
            def _(pe):
                pe.wait_ge(const_in, 64)
                pe.wait_ge(tab_ready, 1)
                nc.tensor.matmul(side[0][0:BIAS_HEADS, :], tab[0:33, :], onehot[0:33, 0:SEQ], start=True, stop=True)
                nc.tensor.matmul(side[1][0:BIAS_HEADS, 0:P], tab[0:33, :], onehot[0:33, SEQ:LINE], start=True,
                                 stop=True).then_inc(line_made, 1)

            @block.vector
            def _(dve):
                dve.wait_ge(line_made, 1)
                nc.vector.tensor_copy(line[0:BIAS_HEADS, 0:SEQ], side[0][0:BIAS_HEADS, :]).then_inc(line_read, 1)
                nc.vector.tensor_copy(line[0:BIAS_HEADS, SEQ:LINE],
                                      side[1][0:BIAS_HEADS, 0:P]).then_inc(line_read, 1)

        def bias_lines(head, n):
            return bass.AP(lines.tensor, head * P * LINE + P - 1, [[LINE - 1, P], [P * LINE, n], [1, SEQ]])

        raw_full = [sem(f"raw_full{b}") for b in range(SLOTS)]
        params_in, w2_in, emb_in = (sem(n) for n in ("params_in", "w2_in", "emb_in"))
        w1_in = [sem(f"w1_in{b}") for b in range(W1_SLOTS)]
        shift_in = [sem("shift_in_keys"), sem("shift_in_values")]
        bias_in = [sem("bias_in_nsa"), sem("bias_in_diff")]
        line_in, line_out = sem("line_in"), sem("line_out")
        cleared = [line_in, line_out, *raw_full, params_in, w2_in, emb_in, *w1_in, *shift_in, *bias_in]
        counts = Counts(nc, ctx, known)
        tick, done, freed = counts.tick, counts.done, counts.freed

        def bank_of(content):
            if not known:
                return main[0]
            which, n = known["bank"][content]
            return (main, side)[which][n % 4]

        def slot_of(name):
            return known["slot"][name] if known else 0

        def source(key, layer):
            if key[0] in TILES:
                return a["w_in_t"][layer, TILES.index(key[0])]
            if key[0].endswith("_down"):
                lo, hi = THIRDS[key[2]]
                return a[key[0]][layer, key[1], :, lo * P:hi * P]
            return a[key[0]][layer, key[1]]

        with nc.Fori(0, DEPTH) as layer:
            with nc.Block() as block:
                @block.sync
                def _(sp):
                    sp.dma_start(cols[:, 0:NPARAM], a["params"][layer]).then_inc(params_in, 16)
                    sp.dma_start(cols[:, NPARAM:NCOLS], a["layer_consts"][layer]).then_inc(params_in, 16)
                    for c, key in enumerate(CHUNKS):
                        if c == LINES_IN_AT:
                            sp.dma_start(line[0:BIAS_HEADS, :], line_once).then_inc(line_in, 16)
                        if c == LINES_OUT_AT:
                            sp.wait_ge(line_in, 16)
                            sp.dma_start(lines, line[0:BIAS_HEADS, None, :].broadcast_to([BIAS_HEADS, P, LINE])
                                         ).then_inc(line_out, 16)
                        if c >= SLOTS:
                            sp.wait_ge(*done("weights_lo", c - SLOTS))
                        sp.dma_start(raw[:, c % SLOTS, 0:chunk_width(key)],
                                     source(key, layer)).then_inc(raw_full[c % SLOTS], 16)

                @block.gpsimd
                def _(pool):
                    pool.wait_ge(*done("product", ("ffn1_down", KT - 1, 2)))
                    pool.wait_ge(*done("h_lo", "ffn1", FT - 1))
                    nc.gpsimd.memset(w2p[:], 0.0).then_inc(*tick("zeros", "w2p"))
                    nc.gpsimd.memset(kc[:], 0.0).then_inc(*tick("zeros", "kc"))
                    nc.gpsimd.memset(vc[:], 0.0).then_inc(*tick("zeros", "vc"))
                    nc.gpsimd.memset(hv[:], 0.0).then_inc(*tick("zeros", "hv"))
                    for p in range(3):
                        for lev in range(LEVELS):
                            g = p * LEVELS + lev
                            pool.wait_ge(*done("decay", p, lev))
                            if g == 0:
                                pool.wait_ge(*done("q_silu"))
                            if lev == 0:
                                pool.wait_ge(*done("hgrn_k", p))
                            if g >= 2:
                                pool.wait_ge(*done("hgrn_scores", g - 2, 1))
                            size = 1 << lev
                            e, o = ev[:, g % 2, :], zv[:, g % 2, :]
                            cut = "p (b two l) -> p b two l"
                            for which, operand in ((0, hf[:, p, :]), (1, hq[:, p, :])):
                                nc.gpsimd.tensor_tensor(
                                    o.rearrange(cut, two=2, l=size)[:, :, which, :],
                                    e.rearrange(cut, two=2, l=size)[:, :, which, :],
                                    operand.rearrange(cut, two=2, l=size)[:, :, which, :],
                                    ALU.mult).then_inc(*tick("decayed", g, which))
                        if p == 0:
                            pool.wait_ge(*done("vc", 1))
                            nc.gpsimd.memset(vpad[:], 0.0).then_inc(*tick("zeros", "vpad"))
                            nc.gpsimd.memset(dv[:], 0.0).then_inc(*tick("zeros", "dv"))

                @block.tensor
                def _(pe):
                    taken = {0: [], 1: []}

                    def take(content, which=1):
                        order = taken[which]
                        n = len(order)
                        if n >= 4:
                            pe.wait_ge(*freed(order[n - 4]))
                        order.append(content)
                        counts.bank[content] = (which, n)
                        return (main, side)[which][n % 4]

                    def three(out, lh, ll, rh, rl, start, stop, **kw):
                        nc.tensor.matmul(out, lh, rh, start=start, stop=False, **kw)
                        nc.tensor.matmul(out, lh, rl, start=False, stop=False, **kw)
                        return nc.tensor.matmul(out, ll, rh, start=False, stop=stop, **kw)

                    def chunk(key):
                        c, n = CHUNK[key], chunk_width(key)
                        pe.wait_ge(*done("weights_lo", c))
                        return wh[:, c % SLOTS, 0:n], wl[:, c % SLOTS, 0:n]

                    def from_x(key, stage=None):
                        out = take(key, 0)
                        h, l = chunk(key)
                        for k in range(KT):
                            if stage:
                                pe.wait_ge(*done("x_lo", stage, k))
                            ks = slice(k * P, (k + 1) * P)
                            mm = three(out[:], h[:, ks], l[:, ks], xh[:, k, :], xl[:, k, :], k == 0, k == KT - 1)
                        mm.then_inc(*tick("product", key))

                    def sum_squares(name):
                        out = take(("squares", name))
                        pe.wait_ge(*done("squares_added", name, KT - 1))
                        nc.tensor.matmul(out[:], const_("ones"), acc[:], start=True,
                                         stop=True).then_inc(*tick("squares", name))

                    def head_squares(name, blocks, n=SEQ):
                        out = take(("head_squares", name))
                        pe.wait_ge(*done("head_sq", name))
                        nc.tensor.matmul(out[:, 0:n], const_(blocks), zs[:, slot_of(name) % 2, 0:n], start=True,
                                         stop=True).then_inc(*tick("head_squares", name))

                    def ffn(name):
                        for ft in range(FT):
                            from_x((name + "_gate", ft), name if ft == 0 else None)
                            if ft == 0:
                                sum_squares(name)
                            from_x((name + "_up", ft))
                        for dt in range(KT):
                            out = take((name + "_down", dt), 0)
                            for third, (lo, hi) in enumerate(THIRDS):
                                key = (name + "_down", dt, third)
                                h, l = chunk(key)
                                for f in range(lo, hi):
                                    if dt == 0:
                                        pe.wait_ge(*done("h_lo", name, f))
                                    fs = slice((f - lo) * P, (f - lo + 1) * P)
                                    mm = three(out[:], h[:, fs], l[:, fs], ffh[:, f, :], ffl[:, f, :], f == 0,
                                               f == FT - 1)
                                if third < 2:
                                    mm.then_inc(*tick("product", key))
                            mm.then_inc(*tick("product", key))

                    nat_outs = {}

                    def project(group, step):
                        names = GROUP_OF[group]
                        if step < len(names):
                            name = names[step]
                            from_x((name,), "mix" if name == TILES[0] else None)
                            if name == TILES[0]:
                                sum_squares("mix")
                            if name == TILES[1]:
                                out = take("turned")
                                pe.wait_ge(*done("factor", "mix"))
                                for t in range(QT):
                                    ts = slice(t * P, (t + 1) * P)
                                    mm = nc.tensor.transpose(out[:, ts], rb[:, ts], const_("ident"))
                                mm.then_inc(*tick("turned"))
                        elif group in NAT:
                            w, c = NAT[group], step - len(names)
                            if c == 0:
                                nat_outs[group] = [take(("nat" + group, t, "out"), 0) for t in range(QT)]
                            h, l = chunk(("nat" + group, c))
                            for t in range(QT):
                                ts = slice(t * P, (t + 1) * P)
                                for kk in range(2):
                                    k, ks = 2 * c + kk, slice(kk * w, (kk + 1) * w)
                                    mm = three(nat_outs[group][t][:, 0:w], xh[:, k, ts], xl[:, k, ts], h[:, ks],
                                               l[:, ks], k == 0, k == KT - 1)
                            mm.then_inc(*tick("product", ("nat" + group, c)))
                        if 0 < step <= len(names) and names[step - 1] in NORMED:
                            name = names[step - 1]
                            head_squares(name, "sum32" if name[0] == "d" else "sum64")

                    def level(p, lev):
                        g = p * LEVELS + lev
                        if lev < 0:
                            pe.wait_ge(*done("q_silu"))
                            pe.wait_ge(*done("hgrn_k", p))
                        else:
                            pe.wait_ge(*done("decayed", g, 1))
                        for hh in range(2):
                            out = take(("h", p, lev, hh))
                            rows = slice(64 * hh, 64 * hh + 64)
                            first = hf[rows, p, :] if lev < 0 else zv[rows, g % 2, :]
                            second = hq[rows, p, :] if lev < 0 else zv[rows, g % 2, :]
                            if lev < 7:
                                parts = [(t * P, t * P, t * P, P) for t in range(QT)]
                            elif lev == 7:
                                parts = [(t * P, 2 * t * P, (2 * t + 1) * P, P) for t in range(2)]
                            else:
                                parts = [(2 * t * P, t * P, 2 * P, 2 * P) for t in range(2)]
                            for o, s, t, w in parts:
                                mm = nc.tensor.matmul(out[:, o:o + w], first[:, s:s + P], second[:, t:t + w],
                                                      start=True, stop=True)
                            mm.then_inc(*(tick("hgrn_scores", g, hh) if lev >= 0 else tick("hgrn_same", p, hh)))

                    def hgrn_values(p):
                        out = take(("hgrn", p), 0)
                        pe.wait_ge(*freed(("h", p, 6, 1)))
                        pe.wait_ge(*freed(("h", p, 8, 1)))
                        for hh in range(2):
                            for j in range(QT):
                                v = hv[:, j, p, 2 * hh:2 * hh + 2, :].rearrange("p a d -> p (a d)")
                                mm = nc.tensor.matmul(out[:, j * P:(j + 1) * P], v,
                                                      sdiag[:, hh, j * P:(j + 1) * P],
                                                      start=(hh == 0 and j == 0),
                                                      stop=False, skip_group_check=True)
                                if j < QT - 1:
                                    o = (0, 3, 5)[j] * P
                                    mm = nc.tensor.matmul(out[:, (j + 1) * P:SEQ], v,
                                                          soff[:, hh, o:o + (QT - 1 - j) * P], start=False,
                                                          stop=False, skip_group_check=True)
                        mm.then_inc(*tick("hgrn_values", p))

                    def hgrn():
                        for p in range(3):
                            for lev in range(-1, LEVELS):
                                level(p, lev)
                                if p and lev == 0:
                                    head_squares(("hgrn", p - 1), "sum64")
                                if (p, lev) in BESIDE_HGRN:
                                    project("A", BESIDE_HGRN[p, lev])
                                if (p, lev) == (2, 2):
                                    compressed_scores()
                                if (p, lev) == (2, 7):
                                    turn_compressed()
                            hgrn_values(p)

                    n2 = 2 * NCMP
                    hidden = {}

                    def cmp_part(k):
                        kv = k // 4
                        if k % 4 == 0:
                            hidden[kv] = take(("hidden", kv))
                            pe.wait_ge(*done("windows", kv))
                        pe.wait_ge(w1_in[k % W1_SLOTS], 16 * (k // W1_SLOTS + 1))
                        for m in range(4 * (k % 4), 4 * (k % 4) + 4):
                            mm = nc.tensor.matmul(hidden[kv][0:n2, 0:CMP_HIDDEN], w2c[:, m, :],
                                                  w1[:, k % W1_SLOTS, m % 4, :],
                                                  start=(m == 0), stop=(m == PAIRS - 1))
                        mm.then_inc(*tick("cmp_part", k))

                    def cmp_turn(kv):
                        out = take(("hiddenT", kv))
                        pe.wait_ge(*done("cmp_gelu", kv))
                        for k in range(2):
                            mm = nc.tensor.transpose(out[:, k * n2:(k + 1) * n2], hid[0:n2, k * P:(k + 1) * P],
                                                     const_("ident")[0:n2, 0:n2])
                        mm.then_inc(*tick("cmp_turned", kv))

                    def cmp_make(kv):
                        out = take(("compressed", kv))
                        pe.wait_ge(*freed(("hiddenT", kv)))
                        pe.wait_ge(*done("w2_padded", kv))
                        for g in range(2):
                            for k in range(2):
                                pad = w2p[:, kv, k, 1 - g:3 - g, :].rearrange("p a d -> p (a d)")
                                part = hidT[:, k, g * NCMP:(g + 1) * NCMP]
                                if kv == 0:
                                    mm = nc.tensor.matmul(out[:, CPAD * g:CPAD * g + NCMP], pad, part,
                                                          start=(k == 0), stop=(k == 1))
                                else:
                                    mm = nc.tensor.matmul(out[CPAD * g:CPAD * g + NCMP, 0:P], part, pad,
                                                          start=(k == 0), stop=(k == 1))
                        mm.then_inc(*tick("cmp_made", kv))

                    def group_c():
                        for step in range(STEPS["C"]):
                            project("C", step)
                            if step == 5:
                                cmp_turn(0)
                            if step == 6:
                                cmp_make(0)
                            if step == 7:
                                head_squares("kc", "sum64", 2 * CPAD)
                            for k in range(8):
                                if CMP_PART_AT[k] == step:
                                    cmp_part(k)
                            if step == 9:
                                cmp_turn(1)
                            if step == 10:
                                cmp_make(1)

                    def compressed_scores():
                        pe.wait_ge(*done("kc"))
                        pe.wait_ge(*done("normed", "nq2", 0))
                        for part, rs in enumerate(((0, 1), (2,))):
                            out = take(("cmp_scores", part))
                            for n, (r, i) in enumerate((r, i) for r in rs for i in range(QT)):
                                mm = nc.tensor.matmul(out[:, n * 2 * CPAD:(n + 1) * 2 * CPAD],
                                                      q[:, r, i * P:(i + 1) * P], kc[:], start=True, stop=True)
                            mm.then_inc(*tick("cmp_scores", part))

                    def turn_compressed():
                        pe.wait_ge(*done("cmp_probs"))
                        for r in range(3):
                            out = take(("cmp_turn", r))
                            for i in range(QT):
                                mm = nc.tensor.transpose(out[0:2 * CPAD, i * P:(i + 1) * P], cp[:, r * QT + i, :],
                                                         const_("ident"))
                            mm.then_inc(*tick("cmp_probsT", r))

                    def nsa():
                        outs = {}
                        for n in range(14):
                            if n < 12:
                                r, g, b = n // 4, n // 2 % 2, n % 2
                                for i in range(QT):
                                    out = take(("s", n, i))
                                    nc.tensor.matmul(out[:, 0:(i + 1) * P], q[:, r, i * P:(i + 1) * P],
                                                     kpad[:, b, g, 0:(i + 1) * P], start=True,
                                                     stop=True).then_inc(*tick("scores", n, i))
                                if n % 4 == 0:
                                    outs[r] = take(("nsa", r), 0)
                                    pe.wait_ge(*freed(("cmp_turn", r)))
                                    pe.wait_ge(*done("vc", 1))
                                    nc.tensor.matmul(outs[r][:], vc[0:2 * CPAD, :], mixed[0:2 * CPAD, r, :],
                                                     start=True, stop=False, skip_group_check=True)
                            if n >= 2:
                                m = n - 2
                                r, g, b = m // 4, m // 2 % 2, m % 2
                                for j in range(QT):
                                    pe.wait_ge(*freed(("t", m, j)))
                                    v = vpad[:, b, j, 2 * g:2 * g + 2, :].rearrange("p a d -> p (a d)")
                                    mm = nc.tensor.matmul(outs[r][:, j * P:SEQ], v,
                                                          probsT[:, m % 2, col0(j):col0(j + 1)], start=False,
                                                          stop=False, skip_group_check=True)
                                mm.then_inc(*tick("values_used", m))
                            if n == 0:
                                head_squares(("hgrn", 2), "sum64")
                            if n in BESIDE_NSA:
                                project("B", BESIDE_NSA[n])
                            if 1 <= n <= 12:
                                m = n - 1
                                for j in range(QT):
                                    out = take(("t", m, j))
                                    pe.wait_ge(*done("probs_scaled", m, QT - 1))
                                    for i in range(j, QT):
                                        at = row0(i) + j * P
                                        mm = nc.tensor.transpose(out[:, i * P:(i + 1) * P],
                                                                 probs[:, m % 2, at:at + P], const_("ident"))
                                    mm.then_inc(*tick("turned_probs", m, j))

                    def diff():
                        outs = {}
                        for n in range(DIFF_HEADS + 2):
                            if n < DIFF_HEADS:
                                for m in range(2):
                                    for i in range(QT):
                                        out = take(("ds", n, m, i))
                                        nc.tensor.matmul(out[:, 0:(i + 1) * P], dq[:, n // 2, i * P:(i + 1) * P],
                                                         dkp[:, n // 2, 2 * (n % 2) + m, 0:(i + 1) * P], start=True,
                                                         stop=True).then_inc(*tick("dscores", n, m, i))
                                if n % 2 == 0:
                                    outs[n // 2] = take(("diff", n // 2), 0)
                            if n >= 2:
                                d = n - 2
                                for j in range(QT):
                                    pe.wait_ge(*freed(("dt", d, j)))
                                    v = dv[:, j, d // 2, 2 * (d % 2):2 * (d % 2) + 2, :].rearrange("p a d -> p (a d)")
                                    mm = nc.tensor.matmul(outs[d // 2][:, j * P:SEQ], v,
                                                          dpT[:, col0(j):col0(j + 1)],
                                                          start=(d % 2 == 0 and j == 0), stop=False,
                                                          skip_group_check=True)
                                mm.then_inc(*tick("dvalues_used", d))
                            if 1 <= n <= DIFF_HEADS:
                                d = n - 1
                                for j in range(QT):
                                    out = take(("dt", d, j))
                                    pe.wait_ge(*done("dprobs", d, QT - 1))
                                    for i in range(j, QT):
                                        at = row0(i) + j * P
                                        mm = nc.tensor.transpose(out[:, i * P:(i + 1) * P], dp[:, d % 2, 0, at:at + P],
                                                                 const_("ident"))
                                    mm.then_inc(*tick("dturned_probs", d, j))

                    def products_out():
                        early, late = MIX_ORDER[:6], MIX_ORDER[6:]
                        outs = {}

                        def part(dt, ks):
                            h, l = chunk(("wout", dt))
                            for k in ks:
                                if dt == 0:
                                    pe.wait_ge(*done("x_lo", "mixed", k))
                                w = slice(k * P, (k + 1) * P)
                                mm = three(outs[dt][:], h[:, w], l[:, w], xh[:, k, :], xl[:, k, :],
                                           k == MIX_ORDER[0], k == MIX_ORDER[-1])
                            return mm

                        for dt in range(2):
                            outs[dt] = take(("wout", dt), 0)
                            part(dt, early)
                            head_squares(("diff", dt), "sum64")
                        for dt in range(2):
                            part(dt, late).then_inc(*tick("product", ("wout", dt)))
                        for dt in range(2, KT):
                            outs[dt] = take(("wout", dt), 0)
                            part(dt, MIX_ORDER).then_inc(*tick("product", ("wout", dt)))

                    ffn("ffn1")
                    group_c()
                    hgrn()
                    nsa()
                    diff()
                    products_out()
                    ffn("ffn2")
                    for h2 in range(2):
                        key = ("ple_proj", h2)
                        h, l = chunk(key)
                        pe.wait_ge(*done("emb_lo", 1))
                        for d in range(4):
                            out = take(("ple_out", 4 * h2 + d), 0)
                            for k in range(2):
                                ks = slice((2 * d + k) * P, (2 * d + k + 1) * P)
                                mm = three(out[:], h[:, ks], l[:, ks], embh[:, k, :], embl[:, k, :], k == 0, k == 1)
                            mm.then_inc(*(tick("product", key) if d == 3 else tick("product", key, d)))
                        sum_squares(("ple", "post")[h2])
                    for dt in range(KT):
                        from_x(("ple_gate", dt), "ple" if dt == 0 else None)

                @block.scalar
                def _(act):
                    at = {"hi": 0, "logs": False}

                    def log_tables():
                        if not at["logs"]:
                            nc.scalar.preload_act_table_set("natural_log_exp_and_others")
                            at["logs"] = True

                    def split(upto):
                        while at["hi"] <= min(upto, len(CHUNKS) - 1):
                            c = at["hi"]
                            n = chunk_width(CHUNKS[c])
                            act.wait_ge(raw_full[c % SLOTS], 16 * (c // SLOTS + 1))
                            if c >= SLOTS:
                                act.wait_ge(*done("product", CHUNKS[c - SLOTS]))
                            nc.scalar.activation(wh[:, c % SLOTS, 0:n], raw[:, c % SLOTS, 0:n],
                                                 ACT.Copy).then_inc(*tick("weights_hi", c))
                            at["hi"] += 1

                    def split_x(stage, gain, k):
                        nc.scalar.activation(xh[:, k, :], x[:, k, :], ACT.Identity, bias=0.0,
                                             scale=col(gain, k)).then_inc(*tick("x_hi", stage, k))

                    def square(norm, k, operand):
                        n = NORMS.index(norm) * KT + k
                        if n >= 2:
                            m = n - 2
                            act.wait_ge(*done("squares_added", NORMS[m // KT], max(m % KT, 1)))
                        nc.scalar.activation(sq[:, k % 2, :], operand,
                                             ACT.Square).then_inc(*tick("squared", norm, k))

                    def factor(name, out):
                        log_tables()
                        act.wait_ge(*done("squares", name))
                        nc.scalar.activation(out, bank_of(("squares", name))[:], ACT.Ln, bias=const_("eps"),
                                             scale=1.0 / D_MODEL).then_inc(
                                                 *tick("factor_ln", name, frees=("squares", name)))
                        act.wait_ge(*done("factor_ln", name))
                        nc.scalar.activation(out, out, ACT.Exp, scale=-0.5).then_inc(*tick("factor", name))

                    norm_order = []

                    def head_square(name, operand, n=SEQ):
                        k = len(norm_order)
                        if k >= 2:
                            act.wait_ge(*done("head_squares", norm_order[k - 2]))
                        norm_order.append(name)
                        counts.slot[name] = k
                        nc.scalar.activation(zs[:, k % 2, 0:n], operand, ACT.Square).then_inc(*tick("head_sq", name))

                    def head_factor(name, width, n=SEQ):
                        log_tables()
                        key = ("head_squares", name)
                        k = norm_order.index(name)
                        out = rn[k % 2][:, 0:n]
                        act.wait_ge(*done(*key))
                        if k >= 2:
                            act.wait_ge(*done(*NORM_READER[norm_order[k - 2]]))
                        nc.scalar.activation(out, bank_of(key)[:, 0:n], ACT.Ln, bias=const_("eps"),
                                             scale=1.0 / width).then_inc(*tick("head_ln", name, frees=key))
                        act.wait_ge(*done("head_ln", name))
                        nc.scalar.activation(out, out, ACT.Exp, scale=-0.5).then_inc(*tick("head_factor", name))

                    def ffn(name, nxt, gain):
                        for ft in range(FT + 1):
                            at["logs"] = at["logs"] and ft == 0
                            if ft < FT:
                                c = CHUNK[(name + "_gate", ft)]
                                split(c + AHEAD)
                                if ft == 0:
                                    factor(name, rb[:])
                                act.wait_ge(*done("gate_scaled", name, ft))
                                nc.scalar.activation(fg[:, ft % 2, :], fg[:, ft % 2, :],
                                                     ACT.Silu).then_inc(*tick("gate_silu", name, ft))
                                split(c + 1 + AHEAD)
                            if ft:
                                act.wait_ge(*done("h", name, ft - 1))
                                nc.scalar.activation(ffh[:, ft - 1, :], fu[:, (ft - 1) % 2, :],
                                                     ACT.Copy).then_inc(*tick("h_hi", name, ft - 1))
                            if name == "ffn1" and ft == 1:
                                act.wait_ge(*done("exponents"))
                                nc.scalar.activation(sm("e", 0, 8), sm("e", 0, 8),
                                                     ACT.Exp).then_inc(*tick("exponentials"))
                                act.wait_ge(*done("logarithm_of"))
                                nc.scalar.activation(sm("lc", 0, 6), sm("lc", 0, 6),
                                                     ACT.Ln).then_inc(*tick("logarithms"))
                        for dt in range(KT):
                            for third in range(3):
                                split(CHUNK[(name + "_down", dt, third)] + AHEAD)
                            act.wait_ge(*done("x_new", name, dt))
                            split_x(nxt, gain, dt)
                            square(nxt, dt, x[:, dt, :])

                    def project(group, step):
                        names = GROUP_OF[group]
                        if step < len(names):
                            name = names[step]
                            split(CHUNK[(name,)] + AHEAD)
                            if name == TILES[0]:
                                factor("mix", rb[:])
                            if name in NORMED:
                                act.wait_ge(*done("scaled", name))
                                head_square(name, z[:, Z_SLOT[name], :])
                        else:
                            split(CHUNK[("nat" + group, step - len(names))] + AHEAD)
                        if 0 < step <= len(names) and names[step - 1] in NORMED:
                            name = names[step - 1]
                            head_factor(name, DIFF_QK if name[0] == "d" else HEAD)
                        if group in NAT and step == len(names) + 3:
                            act.wait_ge(*done("product", ("nat" + group, 3)))
                            act.wait_ge(*done("factor_turned"))
                            act.wait_ge(*done("zeros", "hv" if group == "C" else "dv"))
                            for t in range(QT):
                                key = ("nat" + group, t, "out")
                                o = bank_of(key)

                                def heads(n):
                                    return o[:, n * P:(n + 1) * P].rearrange("p (g d) -> p g d", g=2)

                                if group == "C":
                                    for p in range(3):
                                        nc.scalar.activation(hv[:, t, p, 0:4:3, :], heads(p), ACT.Copy,
                                                             scale=sm("rt", t)).then_inc(*tick("values", "C", t, p))
                                    nc.scalar.activation(gates[:, t, :], o[:, 384:402], ACT.Copy,
                                                         scale=sm("rt", t)).then_inc(
                                                             *tick("values", "C", t, 3, frees=key))
                                else:
                                    for b in range(2):
                                        nc.scalar.activation(vpad[:, b, t, 0:4:3, :], heads(b), ACT.Copy,
                                                             scale=sm("rt", t)).then_inc(*tick("values", "A", t, b))
                                    for b in range(2):
                                        nc.scalar.activation(dv[:, t, b, 0:4:3, :], heads(2 + b), ACT.Copy,
                                                             scale=sm("rt", t)).then_inc(
                                            *tick("values", "A", t, 2 + b, frees=key if b else None))
                            if group == "C":
                                log_tables()
                                act.wait_ge(*done("values", "C", QT - 1, 3))
                                nc.scalar.activation(gates[:], gates[:], ACT.Exp,
                                                     scale=-1.0).then_inc(*tick("gate_exp"))

                    def forget_gate(p):
                        log_tables()
                        if p:
                            act.wait_ge(*done("log_forget", p - 1))
                        f = hf[:, p, :]
                        act.wait_ge(*done("scaled", f"hf{p}"))
                        nc.scalar.activation(ta[:], f, ACT.Abs).then_inc(*tick("forget", p, 0))
                        act.wait_ge(*done("forget", p, 0))
                        nc.scalar.activation(ta[:], ta[:], ACT.Exp, scale=-1.0).then_inc(*tick("forget", p, 1))
                        act.wait_ge(*done("forget", p, 1))
                        nc.scalar.activation(ta[:], ta[:], ACT.Ln,
                                             bias=const_("one")).then_inc(*tick("forget", p, 2))
                        act.wait_ge(*done("log_gap", p))
                        nc.scalar.activation(tb[:], tb[:], ACT.Abs).then_inc(*tick("forget", p, 3))
                        act.wait_ge(*done("forget", p, 3))
                        nc.scalar.activation(tb[:], tb[:], ACT.Exp, scale=-1.0).then_inc(*tick("forget", p, 4))
                        act.wait_ge(*done("forget", p, 4))
                        nc.scalar.activation(tb[:], tb[:], ACT.Ln,
                                             bias=const_("one")).then_inc(*tick("forget", p, 5))
                        act.wait_ge(*done("log_input", p))
                        nc.scalar.activation(f, f, ACT.Exp).then_inc(*tick("forget", p, 6))

                    def decay(g):
                        p, lev = g // LEVELS, g % LEVELS
                        e = ev[:, g % 2, :]
                        if lev < 7:
                            act.wait_ge(*done("exponent", g, 1))
                            nc.scalar.activation(e, e, ACT.Exp).then_inc(*tick("decay", p, lev))
                            return
                        act.wait_ge(*done("cumsum", p, "t01"))
                        if g >= 2:
                            act.wait_ge(*done("decayed", g - 2, 1))
                        c = cum[:, p, :]
                        tot = [cum[:, p, (t + 1) * P - 1:(t + 1) * P] for t in range(QT)]
                        before = {0: tot[0], 2: tot[2]} if lev == 7 else {0: sm("t01", p), 1: tot[1]}
                        behind = {1: 0.0, 3: 0.0} if lev == 7 else {2: 0.0, 3: tot[2]}
                        for t in range(QT):
                            ts = slice(t * P, (t + 1) * P)
                            if t in before:
                                ins = nc.scalar.activation(e[:, ts], c[:, ts], ACT.Exp, bias=before[t],
                                                           scale=-1.0)
                            else:
                                ins = nc.scalar.activation(e[:, ts], c[:, ts], ACT.Exp, bias=behind[t])
                            ins.then_inc(*(tick("decay", p, lev) if t == QT - 1 else tick("decay", p, lev, t)))

                    def far_scores(p, lev):
                        parts = ((0, 0, 1), (5, 1, 2)) if lev == 7 else ((1, 0, 2), (3, 2, 4))
                        for hh in range(2):
                            key = ("h", p, lev, hh)
                            act.wait_ge(*done("hgrn_scores", p * LEVELS + lev, hh))
                            if p:
                                act.wait_ge(*done("hgrn_values", p - 1))
                            else:
                                act.wait_ge(*done("log_forget", 2))
                            for n, (to, lo, hi) in enumerate(parts):
                                nc.scalar.activation(
                                    soff[:, hh, to * P:(to + hi - lo) * P], bank_of(key)[:, lo * P:hi * P],
                                    ACT.Copy).then_inc(*tick("far_scores", p, lev, hh, n,
                                                             frees=key if n else None))

                    def hgrn_square(p):
                        act.wait_ge(*done("hgrn_values", p))
                        head_square(("hgrn", p), bank_of(("hgrn", p))[:])

                    def hgrn():
                        log_tables()
                        for p in range(3):
                            for lev in range(-1, LEVELS):
                                g = p * LEVELS + lev
                                if lev >= 0 and g + 2 < 3 * LEVELS:
                                    decay(g + 2)
                                if p and lev == -1:
                                    hgrn_square(p - 1)
                                if p and lev == 0:
                                    head_factor(("hgrn", p - 1), HEAD)
                                if lev >= 7:
                                    far_scores(p, lev)
                                if (p, lev) == (2, 7):
                                    keep_compressed()
                                if (p, lev) in BESIDE_HGRN:
                                    project("A", BESIDE_HGRN[p, lev])
                                if (p, lev) == (2, 4):
                                    act.wait_ge(*done("cmp_minus_max"))
                                    nc.scalar.activation(cp[:], cp[:], ACT.Exp).then_inc(*tick("cmp_exp"))
                        act.wait_ge(*done("decayed", 3 * LEVELS - 1, 1))
                        act.wait_ge(line_out, 16)
                        act.dma_start(biasA[:], bias_lines(0, NSA_HEADS)).then_inc(bias_in[0], 16)
                        hgrn_square(2)

                    def load_w1(k):
                        act.dma_start(w1[:, k % W1_SLOTS], a["cmp_w1"][layer, k // 4, k % 4]).then_inc(
                            w1_in[k % W1_SLOTS], 16)

                    def load_compression():
                        act.wait_ge(*done("product", ("ffn1_down", KT - 1, 2)))
                        act.wait_ge(*done("h_lo", "ffn1", FT - 1))
                        act.dma_start(w2s[:], a["cmp_w2"][layer]).then_inc(w2_in, 16)
                        for k in range(W1_SLOTS):
                            load_w1(k)

                    def shift_pairs(kv):
                        act.wait_ge(*done("scaled", ("ck", "cv")[kv]))
                        for head in range(2):
                            for odd in range(2):
                                act.dma_start(c2[64 * odd:64 * odd + 64, kv, head, 0:SEQ - odd],
                                              ckv[64 * head:64 * head + 64, kv, odd:SEQ]).then_inc(shift_in[kv], 16)

                    def cmp_gelu(kv):
                        act.wait_ge(*done("cmp_part", 4 * kv + 3))
                        nc.scalar.activation(hid[0:2 * NCMP, :], bank_of(("hidden", kv))[0:2 * NCMP, 0:CMP_HIDDEN],
                                             ACT.Gelu_apprx_tanh).then_inc(
                                                 *tick("cmp_gelu", kv, frees=("hidden", kv)))
                        at["logs"] = False

                    def group_c():
                        load_compression()
                        for step in range(STEPS["C"]):
                            project("C", step)
                            if step < 2:
                                shift_pairs(step)
                            if 3 <= step <= 7:
                                k = step - 3
                                act.wait_ge(*done("cmp_part", k))
                                load_w1(k + W1_SLOTS)
                            if step == 4:
                                cmp_gelu(0)
                            if 3 <= step <= 5:
                                forget_gate(step - 3)
                            if step == 6:
                                act.wait_ge(*done("kc_raw"))
                                head_square("kc", kc[:], 2 * CPAD)
                            if step == 7:
                                head_factor("kc", HEAD, 2 * CPAD)
                            if step == 8:
                                act.wait_ge(*done("scaled", "hq2"))
                                nc.scalar.activation(hq[:], hq[:], ACT.Silu).then_inc(*tick("q_silu"))
                                at["logs"] = False
                                act.wait_ge(*done("cmp_turned", 0))
                                cmp_gelu(1)
                            if step == 10:
                                log_tables()
                                decay(0)
                                decay(1)

                    def keep_compressed():
                        for r in range(3):
                            act.wait_ge(*done("cmp_probsT", r))
                            nc.scalar.activation(mixed[0:2 * CPAD, r, :], bank_of(("cmp_turn", r))[0:2 * CPAD, :],
                                                 ACT.Copy).then_inc(*tick("cmp_kept", r, frees=("cmp_turn", r)))

                    def turned(m):
                        for j in (0, 2):
                            act.wait_ge(*done("turned_probs", m, j))
                            if m >= 2:
                                act.wait_ge(*done("values_used", m - 2))
                            nc.scalar.activation(probsT[:, m % 2, col0(j):col0(j + 1)],
                                                 bank_of(("t", m, j))[:, j * P:SEQ],
                                                 ACT.Copy).then_inc(*tick("probsT_a", m, j, frees=("t", m, j)))

                    def nsa():
                        for n in range(14):
                            if n < 12:
                                for i in range(QT):
                                    act.wait_ge(*done("logits", n, i))
                                    k = 4 * (n % 4) + i
                                    pr = probs[:, n % 2, row0(i):row0(i + 1)]
                                    nc.scalar.activation(pr, pr, ACT.Exp, bias=sm("nm", k), scale=-1.0,
                                                         accum_out=sm("sum", k)).then_inc(*tick("probs", n, i))
                            if n == 11:
                                act.wait_ge(*done("scores", 11, QT - 1))
                                act.dma_start(biasB[:], bias_lines(NSA_HEADS, DIFF_HEADS)).then_inc(bias_in[1], 16)
                            if n >= 5 and n % 4 == 1:
                                r = (n - 5) // 4
                                act.wait_ge(*done("values_used", 4 * r + 3))
                                nc.scalar.activation(mixed[:, r, :], bank_of(("nsa", r))[:],
                                                     ACT.Copy).then_inc(*tick("mixed", r, frees=("nsa", r)))
                            if n == 0:
                                head_factor(("hgrn", 2), HEAD)
                            if n in BESIDE_NSA:
                                project("B", BESIDE_NSA[n])
                            if 1 <= n <= 12:
                                turned(n - 1)

                    def diff():
                        for n in range(DIFF_HEADS + 1):
                            if n < DIFF_HEADS:
                                for m in range(2):
                                    for i in range(QT):
                                        act.wait_ge(*done("dlogits", n, m, i))
                                        k = 8 * (n % 2) + 4 * m + i
                                        pr = dp[:, n % 2, m, row0(i):row0(i + 1)]
                                        nc.scalar.activation(pr, pr, ACT.Exp, bias=sm("nm", k), scale=-1.0,
                                                             accum_out=sm("sum", k)).then_inc(
                                                                 *tick("dexp", n, m, i))
                            if n == 0:
                                act.wait_ge(*done("scaled", "hg2"))
                                nc.scalar.activation(z[:], z[:], ACT.Silu).then_inc(*tick("out_gate"))
                                at["logs"] = False
                                log_tables()
                            if n >= 1:
                                d = n - 1
                                for j in (0, 2):
                                    act.wait_ge(*done("dturned_probs", d, j))
                                    if d >= 1:
                                        act.wait_ge(*done("dvalues_used", d - 1))
                                    nc.scalar.activation(dpT[:, col0(j):col0(j + 1)],
                                                         bank_of(("dt", d, j))[:, j * P:SEQ],
                                                         ACT.Copy).then_inc(*tick("dprobsT_a", d, j,
                                                                                  frees=("dt", d, j)))
                            if n == 1:
                                act.wait_ge(*done("product", ("hg2",)))
                            if 1 <= n <= 3:
                                for k in MIX_ORDER[2 * n - 2:2 * n]:
                                    mixed_hi(k)
                        split(CHUNK[("wout", 0)] + AHEAD)
                        for t in range(2):
                            act.wait_ge(*done("dvalues_used", 2 * t + 1))
                            head_square(("diff", t), bank_of(("diff", t))[:])
                        for t in range(2):
                            head_factor(("diff", t), HEAD)
                        for k in MIX_ORDER[6:]:
                            mixed_hi(k)

                    def mixed_hi(k):
                        act.wait_ge(*done(*MIXED[k]))
                        nc.scalar.activation(xh[:, k, :], mixed[:, k, :], ACT.Copy).then_inc(*tick("x_hi", "mixed", k))

                    act.wait_ge(params_in, 32)
                    act.wait_ge(x_in, 16)
                    for k in range(KT):
                        split_x("ffn1", "ffn1", k)
                        if k < AHEAD:
                            split(k)
                    for k in range(KT):
                        square("ffn1", k, x[:, k, :])
                    ffn("ffn1", "mix", "mix")
                    group_c()
                    hgrn()
                    nsa()
                    diff()
                    for dt in range(KT):
                        split(CHUNK[("wout", dt)] + AHEAD)
                        act.wait_ge(*done("x_new", "out", dt))
                        square("ffn2", dt, x[:, dt, :])
                    act.wait_ge(*done("product", ("wout", KT - 1)))
                    for dt in range(KT):
                        split_x("ffn2", "ffn2", dt)
                    ffn("ffn2", "ple", "ple")
                    act.dma_start(emb[:], a["p"][layer]).then_inc(emb_in, 16)
                    act.wait_ge(emb_in, 16)
                    for k in range(2):
                        nc.scalar.activation(embh[:, k, :], emb[:, k, :], ACT.Copy).then_inc(*tick("emb_hi", k))
                    for dt in range(KT):
                        if dt % 4 == 0:
                            split(CHUNK[("ple_proj", dt // 4)] + AHEAD)
                        key, d = ("ple_proj", dt // 4), dt % 4
                        act.wait_ge(*(done("product", key) if d == 3 else done("product", key, d)))
                        nc.scalar.activation(emby[:, dt, :], bank_of(("ple_out", dt))[:],
                                             ACT.Copy).then_inc(*tick("emb_y", dt, frees=("ple_out", dt)))
                        act.wait_ge(*done("emb_y", dt))
                        square("post", dt, emby[:, dt, :])
                    factor("post", rb2[:])
                    for dt in range(KT):
                        split(CHUNK[("ple_gate", dt)] + AHEAD)
                        if dt == 0:
                            factor("ple", rb[:])
                        act.wait_ge(*done("pgate_scaled", dt))
                        nc.scalar.activation(pg[:, dt % 2, :], pg[:, dt % 2, :],
                                             ACT.Sigmoid).then_inc(*tick("pgate", dt))

                @block.vector
                def _(dve):
                    at = {"lo": 0}

                    def split(upto):
                        while at["lo"] <= min(upto, len(CHUNKS) - 1):
                            c = at["lo"]
                            n = chunk_width(CHUNKS[c])
                            dve.wait_ge(*done("weights_hi", c))
                            nc.vector.tensor_tensor(wl[:, c % SLOTS, 0:n], raw[:, c % SLOTS, 0:n],
                                                    wh[:, c % SLOTS, 0:n], ALU.subtract).then_inc(
                                                        *tick("weights_lo", c))
                            at["lo"] += 1

                    def split_x(stage, gain, k):
                        dve.wait_ge(*done("x_hi", stage, k))
                        nc.vector.scalar_tensor_tensor(out=xl[:, k, :], in0=x[:, k, :], scalar=col(gain, k),
                                                       in1=xh[:, k, :], op0=ALU.mult,
                                                       op1=ALU.subtract).then_inc(*tick("x_lo", stage, k))

                    def add_square(norm, k):
                        if k == 0:
                            return
                        dve.wait_ge(*done("squared", norm, k))
                        if k == 1:
                            if norm != NORMS[0]:
                                dve.wait_ge(*done("squares", NORMS[NORMS.index(norm) - 1]))
                            ins = nc.vector.tensor_tensor(acc[:], sq[:, 0, :], sq[:, 1, :], ALU.add)
                        else:
                            dve.wait_ge(*done("squares_added", norm, k - 1))
                            ins = nc.vector.tensor_tensor(acc[:], acc[:], sq[:, k % 2, :], ALU.add)
                        ins.then_inc(*tick("squares_added", norm, k))

                    def link(ins):
                        at["link"] = at.get("link", 0) + 1
                        ins.then_inc(*tick("link", at["link"]))
                        dve.wait_ge(*done("link", at["link"]))

                    def small_exponents():
                        dve.wait_ge(params_in, 32)
                        V = nc.vector
                        V.tensor_scalar(sm("gq"), col("nq"), HEAD ** -0.5, None, ALU.mult).then_inc(*tick("gains", 0))
                        V.tensor_scalar(sm("gdq"), col("dq"), DIFF_QK ** -0.5, None,
                                        ALU.mult).then_inc(*tick("gains", 1))
                        for b in range(2):
                            V.tensor_scalar(sm("gk", 2 * b, 2), const_("half"), col("nk", 1 + b), None,
                                            ALU.mult).then_inc(*tick("gains", 2 + b))
                        V.tensor_scalar(sm("gdk", 0, 4), const_("quarter"), col("dk"), None,
                                        ALU.mult).then_inc(*tick("gains", 4))
                        V.tensor_scalar(sm("gsub"), col("subln"), col("sub0"), None,
                                        ALU.mult).then_inc(*tick("gains", 5))
                        lam = cols[:, COLS["lam"][0]:COLS["lam"][0] + 128].rearrange("p (a b d) -> p a b d", a=2, b=2)
                        l2 = sm("lam2", 0, 64).rearrange("p (a d) -> p a d", a=2)
                        V.tensor_tensor(sm("max", 0, 3), col("lb", 0, 3), col("lb", 3, 3),
                                        ALU.max).then_inc(*tick("gains", 6))
                        link(V.tensor_tensor(l2, lam[:, :, 0, :], lam[:, :, 1, :], ALU.mult))
                        V.tensor_reduce(sm("e", 6, 2), l2, AX.X, ALU.add).then_inc(*tick("gains", 7))
                        V.tensor_tensor(sm("e", 0, 3), col("lb", 0, 3), sm("max", 0, 3),
                                        ALU.subtract).then_inc(*tick("gains", 8))
                        V.tensor_tensor(sm("e", 3, 3), col("lb", 3, 3), sm("max", 0, 3),
                                        ALU.subtract).then_inc(*tick("exponents"))

                    def small_logarithms():
                        V = nc.vector
                        dve.wait_ge(*done("exponentials"))
                        link(V.tensor_tensor(sm("nlam"), sm("e", 7), sm("e", 6), ALU.subtract))
                        V.tensor_scalar(sm("nlam"), sm("nlam"), col("lam0"), None,
                                        ALU.subtract).then_inc(*tick("gains", 9))
                        link(V.tensor_tensor(sm("tot", 0, 3), sm("e", 0, 3), sm("e", 3, 3), ALU.add))
                        link(V.reciprocal(sm("rec", 0, 3), sm("tot", 0, 3)))
                        link(V.tensor_tensor(sm("e", 0, 3), sm("e", 0, 3), sm("rec", 0, 3), ALU.mult))
                        link(V.tensor_tensor(sm("e", 3, 3), sm("e", 3, 3), sm("rec", 0, 3), ALU.mult))
                        link(V.tensor_tensor(sm("lb", 0, 3), sm("e", 0, 3), sm("e", 3, 3), ALU.add))
                        link(V.tensor_tensor(sm("lb", 0, 3), sm("lb", 0, 3), sm("e", 0, 3), ALU.subtract))
                        link(V.tensor_scalar(sm("lb", 0, 3), sm("lb", 0, 3), col("flag"), None, ALU.mult))
                        link(V.tensor_scalar(sm("lb", 3, 3), sm("lb", 0, 3), -1.0, 1.0, ALU.mult, ALU.add))
                        V.tensor_scalar(sm("li", 0, 6), sm("lb", 0, 6), 0.0, NEG, ALU.is_le,
                                        ALU.mult).then_inc(*tick("gains", 10))
                        V.tensor_scalar(sm("lc", 0, 6), sm("lb", 0, 6), 2.0 ** -60, None,
                                        ALU.max).then_inc(*tick("logarithm_of"))
                        dve.wait_ge(*done("logarithms"))
                        link(V.tensor_tensor(sm("ab", 0, 6), sm("lc", 0, 6), sm("li", 0, 6), ALU.add))

                    def ffn(name, nxt, gain):
                        for ft in range(FT + 2):
                            c = CHUNK[(name + "_gate", min(ft, FT - 1))]
                            if ft < FT:
                                split(c + AHEAD)
                                dve.wait_ge(*done("product", (name + "_gate", ft)))
                                if ft == 0:
                                    dve.wait_ge(*done("factor", name))
                                if ft >= 2:
                                    dve.wait_ge(*done("h", name, ft - 2))
                                nc.vector.tensor_tensor(fg[:, ft % 2, :], bank_of((name + "_gate", ft))[:], rb[:],
                                                        ALU.mult).then_inc(
                                    *tick("gate_scaled", name, ft, frees=(name + "_gate", ft)))
                            if ft >= 2:
                                f = ft - 2
                                dve.wait_ge(*done("h_hi", name, f))
                                nc.vector.tensor_tensor(ffl[:, f, :], fu[:, f % 2, :], ffh[:, f, :],
                                                        ALU.subtract).then_inc(*tick("h_lo", name, f))
                            if ft < FT:
                                split(c + 1 + AHEAD)
                                dve.wait_ge(*done("product", (name + "_up", ft)))
                                if ft >= 2:
                                    dve.wait_ge(*done("h_lo", name, ft - 2))
                                nc.vector.tensor_tensor(fu[:, ft % 2, :], bank_of((name + "_up", ft))[:], rb[:],
                                                        ALU.mult).then_inc(
                                    *tick("up_scaled", name, ft, frees=(name + "_up", ft)))
                                dve.wait_ge(*done("up_scaled", name, ft))
                                dve.wait_ge(*done("gate_silu", name, ft))
                                nc.vector.tensor_tensor(fu[:, ft % 2, :], fu[:, ft % 2, :], fg[:, ft % 2, :],
                                                        ALU.mult).then_inc(*tick("h", name, ft))
                            if name == "ffn1" and ft == 0:
                                small_exponents()
                            if name == "ffn1" and ft == 1:
                                small_logarithms()
                        for dt in range(KT):
                            for third in range(3):
                                split(CHUNK[(name + "_down", dt, third)] + AHEAD)
                            dve.wait_ge(*done("product", (name + "_down", dt, 2)))
                            nc.vector.scalar_tensor_tensor(out=x[:, dt, :], in0=bank_of((name + "_down", dt))[:],
                                                           scalar=0.5, in1=x[:, dt, :], op0=ALU.mult,
                                                           op1=ALU.add).then_inc(
                                *tick("x_new", name, dt, frees=(name + "_down", dt)))
                            dve.wait_ge(*done("x_new", name, dt))
                            split_x(nxt, gain, dt)
                            add_square(nxt, dt)

                    def scaled(name, out):
                        dve.wait_ge(*done("product", (name,)))
                        nc.vector.tensor_tensor(out, bank_of((name,))[:], rb[:],
                                                ALU.mult).then_inc(*tick("scaled", name, frees=(name,)))

                    def normed(name):
                        zz = z[:, Z_SLOT[name], :]
                        dve.wait_ge(*done("head_factor", name))
                        dve.wait_ge(*done("scaled", name))
                        t = int(name[-1]) if name[-1].isdigit() else 0
                        if name[0] == "d":
                            dve.wait_ge(*done("hgrn_values", 2))
                            dve.wait_ge(*done("cmp_probsT", 2))
                        if name[:2] == "nq":
                            outs = [(q[:, t, :], sm("gq"))]
                        elif name[:2] == "dq":
                            outs = [(dq[:, t, :], sm("gdq"))]
                        elif name in ("sk", "wk"):
                            b = ("sk", "wk").index(name)
                            outs = [(kpad[:, b, g, :], sm("gk", 2 * b + g)) for g in range(2)]
                        else:
                            outs = [(dkp[:, t, g, :], sm("gdk", g)) for g in range(4)]
                        for n, (out, gain) in enumerate(outs):
                            key = ("normed", name, n - len(outs) + 1)
                            nc.vector.scalar_tensor_tensor(out=out, in0=zz, scalar=gain,
                                                           in1=rn[slot_of(name) % 2][:], op0=ALU.mult,
                                                           op1=ALU.mult).then_inc(*tick(*key))

                    def project(group, step):
                        names = GROUP_OF[group]
                        if step < len(names):
                            name = names[step]
                            split(CHUNK[(name,)] + AHEAD)
                            if name == TILES[0]:
                                dve.wait_ge(*done("factor", "mix"))
                            if name[:2] in ("hf", "hq"):
                                scaled(name, {"hf": hf, "hq": hq}[name[:2]][:, int(name[2]), :])
                            elif name in ("ck", "cv"):
                                scaled(name, ckv[:, ("ck", "cv").index(name), :])
                            else:
                                scaled(name, z[:, Z_SLOT[name], :])
                            if name == TILES[1]:
                                dve.wait_ge(*done("turned"))
                                nc.vector.tensor_copy(sm("rt", 0, 4), bank_of("turned")[:, 0:SEQ:P]).then_inc(
                                    *tick("factor_turned", frees="turned"))
                        elif group in NAT:
                            split(CHUNK[("nat" + group, step - len(names))] + AHEAD)
                        if 0 < step <= len(names) and names[step - 1] in NORMED:
                            normed(names[step - 1])

                    def forget_gate(p, half):
                        V = nc.vector
                        f = hf[:, p, :]
                        la, lb = sm("ab", p), sm("ab", 3 + p)
                        if half == 0:
                            dve.wait_ge(*done("forget", p, 2))
                            link(V.scalar_tensor_tensor(out=tb[:], in0=f, scalar=0.0, in1=ta[:], op0=ALU.min,
                                                        op1=ALU.subtract))
                            V.tensor_tensor(f, tb[:], f, ALU.subtract).then_inc(*tick("log_input", p))
                            V.tensor_scalar(tc[:], tb[:], lb, la, ALU.add, ALU.max).then_inc(*tick("log_max", p))
                            V.tensor_scalar(tb[:], tb[:], lb, la, ALU.add,
                                            ALU.subtract).then_inc(*tick("log_gap", p))
                            return
                        dve.wait_ge(*done("forget", p, 5))
                        dve.wait_ge(*done("log_max", p))
                        V.tensor_tensor(tc[:], tc[:], tb[:], ALU.add).then_inc(*tick("log_forget", p))
                        dve.wait_ge(*done("forget", p, 6))
                        V.tensor_scalar(f, f, sm("lb", 3 + p), None, ALU.mult).then_inc(*tick("hgrn_k", p))
                        dve.wait_ge(*done("log_forget", p))
                        for t in range(QT):
                            ts = slice(t * P, (t + 1) * P)
                            V.tensor_tensor_scan(cum[:, p, ts], const_("ones"), tc[:, ts], 0.0, ALU.mult,
                                                 ALU.add).then_inc(*tick("cumsum", p, t))
                        dve.wait_ge(*done("cumsum", p, 1))
                        V.tensor_tensor(sm("t01", p), cum[:, p, P - 1:P], cum[:, p, 2 * P - 1:2 * P],
                                        ALU.add).then_inc(*tick("cumsum", p, "t01"))

                    def exponents(g):
                        V = nc.vector
                        p, lev = g // LEVELS, g % LEVELS
                        if g >= 3 * LEVELS or lev >= 7:
                            return
                        size = 1 << lev
                        c = cum[:, p, :].rearrange("p (b two l) -> p b two l", two=2, l=size)
                        e = ev[:, g % 2, :].rearrange("p (b two l) -> p b two l", two=2, l=size)
                        ref = c[:, :, 0, size - 1:size].broadcast_to([P, SEQ // (2 * size), size])
                        if g >= 2:
                            dve.wait_ge(*done("decayed", g - 2, 1))
                        V.tensor_tensor(e[:, :, 0, :], ref, c[:, :, 0, :],
                                        ALU.subtract).then_inc(*tick("exponent", g, 0))
                        V.tensor_tensor(e[:, :, 1, :], c[:, :, 1, :], ref,
                                        ALU.subtract).then_inc(*tick("exponent", g, 1))

                    def keep(p, lev):
                        V = nc.vector
                        for hh in range(2):
                            out = sdiag[:, hh, :].rearrange("p (t s) -> p t s", t=QT)
                            key = ("h", p, lev, hh)
                            src = bank_of(key)[:].rearrange("p (t s) -> p t s", t=QT)
                            if lev < 0:
                                dve.wait_ge(*done("hgrn_same", p, hh))
                                if p:
                                    dve.wait_ge(*done("hgrn_values", p - 1))
                                eye = const_("ident")[:, None, :].broadcast_to([P, QT, P])
                                ins = V.tensor_tensor(out, src, eye, ALU.mult)
                            else:
                                dve.wait_ge(*done("hgrn_scores", p * LEVELS + lev, hh))
                                dve.wait_ge(*done("near_scores", p, lev - 1, hh))
                                m = lmask[:, lev, :].bitcast(U32)[:, None, :].broadcast_to([P, QT, P])
                                ins = V.copy_predicated(out, m, src)
                            ins.then_inc(*tick("near_scores", p, lev, hh, frees=key))

                    def branch_gates():
                        V = nc.vector
                        dve.wait_ge(*done("gate_exp"))
                        link(V.tensor_scalar(gates[:], gates[:], 1.0, None, ALU.add))
                        link(V.reciprocal(gates[:], gates[:]))
                        link(V.tensor_scalar(gates[:, 0, 0:18:3], gates[:, 0, 0:18:3], const_("live"), None,
                                             ALU.mult))

                    def hgrn():
                        for p in range(3):
                            for lev in range(-1, LEVELS):
                                g = p * LEVELS + lev
                                if lev >= 0:
                                    exponents(g + 2)
                                if lev < 7:
                                    keep(p, lev)
                                if p and lev == 0:
                                    out_norm(("hgrn", p - 1), 4 + p, col("hout"), "hgrn_out", p - 1)
                                if (p, lev) == (0, 0):
                                    branch_gates()
                                if (p, lev) in BESIDE_HGRN:
                                    project("A", BESIDE_HGRN[p, lev])
                                if (p, lev) == (2, 3):
                                    compressed_scores()
                                if (p, lev) == (2, 5):
                                    compressed_probs()

                    def out_norm(key, tile, gain, kind, n):
                        dve.wait_ge(*done("head_factor", key))
                        nc.vector.scalar_tensor_tensor(out=mixed[:, tile, :], in0=bank_of(key)[:], scalar=gain,
                                                       in1=rn[slot_of(key) % 2][:], op0=ALU.mult, op1=ALU.mult).then_inc(
                                                           *tick(kind, n, frees=key))

                    n2 = 2 * NCMP

                    def cmp_windows(kv):
                        V = nc.vector
                        dve.wait_ge(shift_in[kv], 64)
                        if kv:
                            dve.wait_ge(*done("cmp_part", 3))
                        src = bass.AP(c2, kv * 2 * SEQ, [[4 * SEQ, P], [2, PAIRS], [SEQ, 2], [CMP_STRIDE, NCMP]])
                        pos = cols[:, COLS["pos"][0] + kv * PAIRS:COLS["pos"][0] + (kv + 1) * PAIRS]
                        pos = pos[:, :, None].broadcast_to([P, PAIRS, n2])
                        V.tensor_tensor(w2c[:].rearrange("p m (h n) -> p m h n", h=2), src,
                                        pos.rearrange("p m (h n) -> p m h n", h=2),
                                        ALU.add).then_inc(*tick("windows", kv))

                    def cmp_hidden(kv):
                        dve.wait_ge(*done("cmp_turned", kv))
                        if kv:
                            dve.wait_ge(*done("cmp_made", 0))
                        nc.vector.tensor_copy(hidT[:].rearrange("p k n -> p (k n)"),
                                              bank_of(("hiddenT", kv))[:, 0:2 * n2]).then_inc(
                                                  *tick("hidT", kv, frees=("hiddenT", kv)))

                    def group_c():
                        V = nc.vector
                        for step in range(STEPS["C"]):
                            project("C", step)
                            if step == 1:
                                cmp_windows(0)
                            if step == 4:
                                cmp_windows(1)
                            if 4 <= step <= 6:
                                forget_gate(step - 4, 1)
                            if 3 <= step <= 5:
                                forget_gate(step - 3, 0)
                            if step == 2:
                                dve.wait_ge(w2_in, 16)
                                dve.wait_ge(*done("zeros", "vc"))
                                for kv in range(2):
                                    V.tensor_copy(w2p[:, kv, :, 1, :], w2s[:, kv]).then_inc(*tick("w2_padded", kv))
                            if step == 5:
                                cmp_hidden(0)
                            if step == 6:
                                dve.wait_ge(*done("cmp_made", 0))
                                o = bank_of(("compressed", 0))
                                kv3 = kc[:].rearrange("p (g n) -> p g n", g=2)[:, :, 0:NCMP]
                                V.tensor_copy(kv3, o[:, 0:2 * CPAD].rearrange("p (g n) -> p g n", g=2)[:, :, 0:NCMP]
                                              ).then_inc(*tick("kc_raw", frees=("compressed", 0)))
                            if step == 8:
                                dve.wait_ge(*done("kc_raw"))
                                dve.wait_ge(*done("head_factor", "kc"))
                                V.scalar_tensor_tensor(out=kc[:], in0=kc[:], scalar=col("nk", 0),
                                                       in1=rn[slot_of("kc") % 2][:, 0:2 * CPAD], op0=ALU.mult,
                                                       op1=ALU.mult).then_inc(*tick("kc"))
                            if step == 9:
                                cmp_hidden(1)
                                dve.wait_ge(*done("cumsum", 2, "t01"))
                                exponents(0)
                                exponents(1)
                            if step == 10:
                                dve.wait_ge(*done("cmp_made", 1))
                                o = bank_of(("compressed", 1))
                                for g in range(2):
                                    rows = slice(CPAD * g, CPAD * g + NCMP)
                                    V.tensor_copy(vc[rows, :], o[rows, 0:P]).then_inc(
                                        *(tick("vc", g, frees=("compressed", 1)) if g else tick("vc", g)))

                    def compressed_scores():
                        V = nc.vector
                        mask = const_("cmask")
                        for part, (r0, nr) in enumerate(((0, 2), (2, 1))):
                            dve.wait_ge(*done("cmp_scores", part))
                            w = QT * 2 * CPAD
                            V.tensor_tensor(cp[:, r0 * QT:(r0 + nr) * QT, :].rearrange("p (r i) n -> p r (i n)", r=nr),
                                            bank_of(("cmp_scores", part))[:, 0:nr * w].rearrange(
                                                "p (r n) -> p r n", r=nr),
                                            mask[:, None, :].broadcast_to([P, nr, w]), ALU.add).then_inc(
                                                *tick("cmp_masked", part, frees=("cmp_scores", part)))
                        flat = cp[:].rearrange("p a (g n) -> p (a g) n", g=2)
                        dve.wait_ge(*done("cmp_masked", 1))
                        link(V.tensor_reduce(sm("cmax", 0, 24), flat, AX.X, ALU.max))
                        V.tensor_tensor(flat, flat, sm("cmax", 0, 24)[:, :, None].broadcast_to([P, 24, CPAD]),
                                        ALU.subtract).then_inc(*tick("cmp_minus_max"))

                    def compressed_probs():
                        V = nc.vector
                        flat = cp[:].rearrange("p a (g n) -> p (a g) n", g=2)
                        dve.wait_ge(*done("cmp_exp"))
                        link(V.tensor_reduce(sm("csum", 0, 24), flat, AX.X, ALU.add))
                        link(V.reciprocal(sm("csum", 0, 24), sm("csum", 0, 24)))
                        for r in range(3):
                            gate = gates[:, :, 3 * r:3 * r + 10:9]
                            V.tensor_tensor(sm("ccoef", 8 * r, 8).rearrange("p (i g) -> p i g", g=2),
                                            sm("csum", 8 * r, 8).rearrange("p (i g) -> p i g", g=2), gate,
                                            ALU.mult).then_inc(*tick("ccoef", r))
                        dve.wait_ge(*done("ccoef", 2))
                        V.tensor_tensor(flat, flat, sm("ccoef", 0, 24)[:, :, None].broadcast_to([P, 24, CPAD]),
                                        ALU.mult).then_inc(*tick("cmp_probs"))

                    def logits(out, content, bias, k, name, key, n):
                        nc.vector.tensor_tensor_reduce(out=out, in0=bank_of(content)[:, 0:n], in1=bias, scale=-1.0,
                                                       scalar=3e38, op0=ALU.add, op1=ALU.min,
                                                       accum_out=sm("nm", k)).then_inc(
                                                           *tick(name, *key, frees=content))

                    def nsa():
                        V = nc.vector
                        dve.wait_ge(bias_in[0], 16)
                        for n in range(14):
                            if n >= 2:
                                for j in (1, 3):
                                    evacuate(n - 2, j)
                            if 1 <= n <= 12:
                                scale(n - 1)
                            if n < 12:
                                r, g = n // 4, n // 2 % 2
                                for i in range(QT):
                                    dve.wait_ge(*done("scores", n, i))
                                    if n >= 2:
                                        dve.wait_ge(*done("turned_probs", n - 2, QT - 1))
                                    logits(probs[:, n % 2, row0(i):row0(i + 1)], ("s", n, i),
                                           biasA[:, g * GROUP + r, SEQ - (i + 1) * P:SEQ], 4 * (n % 4) + i, "logits",
                                           (n, i), (i + 1) * P)
                            if n == 1:
                                out_norm(("hgrn", 2), 7, col("hout"), "hgrn_out", 2)
                            if n in BESIDE_NSA:
                                project("B", BESIDE_NSA[n])

                    def evacuate(m, j):
                        dve.wait_ge(*done("turned_probs", m, j))
                        if m >= 2:
                            dve.wait_ge(*done("values_used", m - 2))
                        nc.vector.tensor_copy(probsT[:, m % 2, col0(j):col0(j + 1)],
                                              bank_of(("t", m, j))[:, j * P:SEQ]).then_inc(
                                                  *tick("probsT_v", m, j, frees=("t", m, j)))

                    def scale(m):
                        V = nc.vector
                        r, g, b = m // 4, m // 2 % 2, m % 2
                        k = 4 * (m % 4)
                        dve.wait_ge(*done("probs", m, QT - 1))
                        link(V.reciprocal(sm("coef", k, 4), sm("sum", k, 4)))
                        link(V.tensor_tensor(sm("coef", k, 4), sm("coef", k, 4),
                                             gates[:, :, (g * GROUP + r) * 3 + 1 + b], ALU.mult))
                        for i in range(QT):
                            pr = probs[:, m % 2, row0(i):row0(i + 1)]
                            V.tensor_scalar(pr, pr, sm("coef", k + i), None,
                                            ALU.mult).then_inc(*tick("probs_scaled", m, i))

                    def diff():
                        V = nc.vector
                        dve.wait_ge(bias_in[1], 16)
                        for n in range(DIFF_HEADS + 2):
                            if n >= 2:
                                for j in (1, 3):
                                    devacuate(n - 2, j)
                            if 1 <= n <= DIFF_HEADS:
                                d = n - 1
                                k = 8 * (d % 2)
                                dve.wait_ge(*done("dexp", d, 1, QT - 1))
                                link(V.reciprocal(sm("coef", k, 8), sm("sum", k, 8)))
                                link(V.tensor_scalar(sm("coef", k + 4, 4), sm("coef", k + 4, 4), sm("nlam"), None,
                                                     ALU.mult))
                                for i in range(QT):
                                    second = dp[:, d % 2, 1, row0(i):row0(i + 1)]
                                    V.tensor_scalar(second, second, sm("coef", k + 4 + i), None,
                                                    ALU.mult).then_inc(*tick("dsecond", d, i))
                                for i in range(QT):
                                    first = dp[:, d % 2, 0, row0(i):row0(i + 1)]
                                    second = dp[:, d % 2, 1, row0(i):row0(i + 1)]
                                    dve.wait_ge(*done("dsecond", d, i))
                                    V.scalar_tensor_tensor(out=first, in0=first, scalar=sm("coef", k + i), in1=second,
                                                           op0=ALU.mult, op1=ALU.add).then_inc(
                                                               *tick("dprobs", d, i))
                            if n < DIFF_HEADS:
                                for m in range(2):
                                    for i in range(QT):
                                        dve.wait_ge(*done("dscores", n, m, i))
                                        if n >= 2:
                                            dve.wait_ge(*done("dturned_probs", n - 2, QT - 1))
                                        logits(dp[:, n % 2, m, row0(i):row0(i + 1)], ("ds", n, m, i),
                                               biasB[:, n, SEQ - (i + 1) * P:SEQ], 8 * (n % 2) + 4 * m + i,
                                               "dlogits", (n, m, i), (i + 1) * P)
                            if n == 1:
                                dve.wait_ge(*done("out_gate"))
                                for p in range(3):
                                    V.tensor_tensor(mixed[:, 5 + p, :], mixed[:, 5 + p, :],
                                                    z[:, Z_SLOT[f"hg{p}"], :], ALU.mult).then_inc(*tick("gated", p))
                            if 2 <= n <= 4:
                                for k in MIX_ORDER[2 * n - 4:2 * n - 2]:
                                    mixed_lo(k)
                        split(CHUNK[("wout", 0)] + AHEAD)
                        for t in range(2):
                            out_norm(("diff", t), 3 + t, sm("gsub"), "diff_out", t)
                        for k in MIX_ORDER[6:]:
                            mixed_lo(k)

                    def mixed_lo(k):
                        dve.wait_ge(*done("x_hi", "mixed", k))
                        nc.vector.tensor_tensor(xl[:, k, :], mixed[:, k, :], xh[:, k, :],
                                                ALU.subtract).then_inc(*tick("x_lo", "mixed", k))

                    def devacuate(d, j):
                        dve.wait_ge(*done("dturned_probs", d, j))
                        if d >= 1:
                            dve.wait_ge(*done("dvalues_used", d - 1))
                        nc.vector.tensor_copy(dpT[:, col0(j):col0(j + 1)],
                                              bank_of(("dt", d, j))[:, j * P:SEQ]).then_inc(
                                                  *tick("dprobsT_v", d, j, frees=("dt", d, j)))

                    dve.wait_ge(x_in, 16)
                    for k in range(KT):
                        if k < AHEAD:
                            split(k)
                        split_x("ffn1", "ffn1", k)
                    for k in range(KT):
                        add_square("ffn1", k)
                    ffn("ffn1", "mix", "mix")
                    group_c()
                    hgrn()
                    nsa()
                    diff()
                    for dt in range(KT):
                        split(CHUNK[("wout", dt)] + AHEAD)
                        dve.wait_ge(*done("product", ("wout", dt)))
                        nc.vector.tensor_tensor(x[:, dt, :], bank_of(("wout", dt))[:], x[:, dt, :],
                                                ALU.add).then_inc(*tick("x_new", "out", dt, frees=("wout", dt)))
                        add_square("ffn2", dt)
                    for dt in range(KT):
                        dve.wait_ge(*done("x_new", "out", dt))
                        split_x("ffn2", "ffn2", dt)
                    ffn("ffn2", "ple", "ple")
                    for k in range(2):
                        dve.wait_ge(*done("emb_hi", k))
                        nc.vector.tensor_tensor(embl[:, k, :], emb[:, k, :], embh[:, k, :],
                                                ALU.subtract).then_inc(*tick("emb_lo", k))
                    for dt in range(KT):
                        if dt % 4 == 0:
                            split(CHUNK[("ple_proj", dt // 4)] + AHEAD)
                        add_square("post", dt)
                    dve.wait_ge(*done("factor", "post"))
                    for dt in range(KT):
                        nc.vector.scalar_tensor_tensor(out=emby[:, dt, :], in0=emby[:, dt, :], scalar=col("post", dt),
                                                       in1=rb2[:], op0=ALU.mult,
                                                       op1=ALU.mult).then_inc(*tick("emb_normed", dt))
                    for dt in range(KT):
                        split(CHUNK[("ple_gate", dt)] + AHEAD)
                        dve.wait_ge(*done("product", ("ple_gate", dt)))
                        if dt == 0:
                            dve.wait_ge(*done("factor", "ple"))
                        nc.vector.tensor_tensor(pg[:, dt % 2, :], bank_of(("ple_gate", dt))[:], rb[:],
                                                ALU.mult).then_inc(*tick("pgate_scaled", dt, frees=("ple_gate", dt)))
                        dve.wait_ge(*done("pgate", dt))
                        dve.wait_ge(*done("emb_normed", dt))
                        nc.vector.tensor_tensor(pg[:, dt % 2, :], pg[:, dt % 2, :], emby[:, dt, :],
                                                ALU.mult).then_inc(*tick("pgated", dt))
                        dve.wait_ge(*done("pgated", dt))
                        nc.vector.tensor_tensor(x[:, dt, :], x[:, dt, :], pg[:, dt % 2, :],
                                                ALU.add).then_inc(*tick("x_new", "ple", dt))

            with nc.Block() as block:
                @block.sync
                def _(sp):
                    nums = [s.num for s in (*cleared, *counts.sems.values())]
                    assert len(nums) == max(nums) - min(nums) + 1
                    sp.sem_clear(range(min(nums), max(nums) + 1))

        with nc.Block() as block:
            @block.sync
            def _(sp):
                sp.dma_start(a["out"], x[:]).then_inc(x_out, 16)
                sp.wait_ge(x_out, 16)
        return counts.facts()


NORMS = ["ffn1", "mix", "ffn2", "ple", "post"]
MIXED = {**{r: ("mixed", r) for r in range(3)}, **{3 + t: ("diff_out", t) for t in range(2)},
         **{5 + p: ("gated", p) for p in range(3)}}
MIX_ORDER = [0, 1, 2, 5, 6, 7, 3, 4]
NORM_READER = {**{("hgrn", p): ("hgrn_out", p) for p in range(3)}, **{n: ("normed", n, 0) for n in NORMED},
               "kc": ("kc",), **{("diff", t): ("diff_out", t) for t in range(2)}}


def bucket_of(distance):
    n = np.maximum(distance, 0)
    exact = BUCKETS // 2
    nf = np.maximum(n, 1).astype(np.float32)
    far = exact + (np.log(nf / exact) / math.log(MAX_DISTANCE / exact) * (BUCKETS - exact)).astype(np.int32)
    return np.where(n < exact, n, np.minimum(far, BUCKETS - 1))


def shape_constants():
    c = np.zeros((P, NCONST), np.float32)

    def put(name, value):
        at, n = CONST[name]
        c[:, at:at + n] = value

    p = np.arange(P)
    put("ident", np.eye(P))
    put("ones", 1.0)
    put("sum64", p[:, None] // 64 == p[None] // 64)
    put("sum32", p[:, None] // 32 == p[None] // 32)
    put("half", p[:, None] // 64 == np.arange(2))
    put("quarter", p[:, None] // 32 == np.arange(4))
    n = np.arange(CPAD)
    t = np.arange(QT)[None, :, None, None] * P + p[:, None, None, None]
    ok = (n < NCMP) & (CMP_STRIDE * n + CMP_BLOCK - 1 <= t)
    put("cmask", np.where(np.broadcast_to(ok, (P, QT, 2, CPAD)), 0.0, NEG).reshape(P, -1))
    put("live", (p >= CMP_BLOCK - 1)[:, None])
    put("eps", EPS)
    put("one", 1.0)
    distance = SEQ - 1 - np.arange(LINE)
    row = np.where(distance < 0, BUCKETS, bucket_of(distance))
    onehot = (np.arange(BUCKETS + 1)[:, None] == row[None]).astype(np.float32)
    s, t = p[:, None], p[None, :]
    masks = np.zeros((P, 7, P), np.float32)
    for lev in range(7):
        size = 1 << lev
        masks[:, lev] = (s // (2 * size) == t // (2 * size)) & (s // size % 2 == 0) & (t // size % 2 == 1)
    return c, onehot, masks


def lay_out(i):
    D = DEPTH
    out = {}
    out["x"] = i["x"][0].T.reshape(KT, P, SEQ).transpose(1, 0, 2)
    out["p"] = i["p"][:, 0].transpose(0, 2, 1).reshape(D, 2, P, SEQ).transpose(0, 2, 1, 3)
    out["rel_bias"] = i["rel_bias"]
    for name in ("ffn1", "ffn2"):
        for part in ("gate", "up"):
            w = i[f"{name}_w_{part}"].reshape(D, KT, P, FT, P)
            out[f"{name}_{part}"] = w.transpose(0, 3, 2, 1, 4).reshape(D, FT, P, WIDE)
        w = i[f"{name}_w_down"].reshape(D, FT, P, KT, P)
        out[f"{name}_down"] = w.transpose(0, 3, 2, 1, 4).reshape(D, KT, P, FT * P)
    w = i["w_in"]
    widths = (384, 128, 128, 128, 128, 128, 128, 18, 256, 256, 256, 384, 384, 384, 384)
    names = ("nq", "ck", "cv", "sk", "sv", "wk", "wv", "ng", "dq", "dk", "dv", "hq", "hf", "hi", "hg")
    cut = dict(zip(names, np.split(w, np.cumsum(widths)[:-1].tolist(), axis=2)))
    nq = cut["nq"].reshape(D, D_MODEL, NSA_KV, GROUP, HEAD).transpose(0, 1, 3, 2, 4).reshape(D, D_MODEL, 384)
    parts = {**cut, "nq": nq}
    tiles = []
    for name in TILES:
        t = int(name[2]) if len(name) == 3 else 0
        tiles.append(parts[name[:2]][:, :, t * P:(t + 1) * P])
    w = np.stack(tiles, 1).reshape(D, len(TILES), KT, P, P)
    out["w_in_t"] = w.transpose(0, 1, 3, 2, 4).reshape(D, len(TILES), P, WIDE)
    for group, list_ in (("C", ("hi", "ng")), ("A", ("sv", "wv", "dv"))):
        w = np.concatenate([cut[n] for n in list_], 2).reshape(D, 4, 2, P, NAT[group])
        out["nat" + group] = w.transpose(0, 1, 3, 2, 4).reshape(D, 4, P, 2 * NAT[group])
    w = i["w_out"]
    nsa = w[:, 0:384].reshape(D, NSA_KV, GROUP, HEAD, D_MODEL).transpose(0, 2, 1, 3, 4).reshape(D, 384, D_MODEL)
    w = np.concatenate([nsa, w[:, 384:]], 1).reshape(D, KT, P, KT, P)
    out["wout"] = w.transpose(0, 3, 2, 1, 4).reshape(D, KT, P, WIDE)
    w = i["ple_w_gate"].reshape(D, KT, P, KT, P)
    out["ple_gate"] = w.transpose(0, 3, 2, 1, 4).reshape(D, KT, P, WIDE)
    w = i["ple_w_proj"].reshape(D, 2, P, 2, 4, P)
    out["ple_proj"] = w.transpose(0, 3, 2, 4, 1, 5).reshape(D, 2, P, WIDE)
    w = i["nsa_cmp_w1"].reshape(D, 2, 4, 4, P, CMP_HIDDEN)
    out["cmp_w1"] = w.transpose(0, 1, 2, 4, 3, 5)
    out["cmp_w2"] = i["nsa_cmp_w2"].reshape(D, 2, 2, P, HEAD).transpose(0, 3, 1, 2, 4)

    def tiled(v, n):
        return np.tile(v, (1, n))[:, :, None]

    by_tile = [i[n].reshape(D, KT, P).transpose(0, 2, 1)
               for n in ("ffn1_norm", "mix_norm", "ffn2_norm", "ple_norm", "ple_post_norm")]
    k_norm = np.concatenate([tiled(i["nsa_k_norm"][:, b], 2) for b in range(3)], 2)
    lb = np.broadcast_to(i["hgrn_lb_logits"].reshape(1, DEPTH * 3, P), (D, DEPTH * 3, P)).transpose(0, 2, 1)
    lam = np.broadcast_to(i["diff_lambda"].reshape(D, 1, 128), (D, P, 128))
    pos = i["nsa_cmp_pos"].reshape(D, 2, PAIRS, P).transpose(0, 3, 1, 2).reshape(D, P, 2 * PAIRS)
    out["params"] = np.concatenate(
        [*by_tile, tiled(i["nsa_q_norm"], 2), k_norm, tiled(i["diff_q_norm"], 4), tiled(i["diff_k_norm"], 4),
         tiled(i["diff_subln"], 2), tiled(i["hgrn_out_norm"], 2), lb, lam, pos], 2)
    lam0 = [0.8 - 0.6 * math.exp(-0.3 * layer) for layer in range(D)]
    rows = np.array([[float(layer > 0), lam0[layer], 1.0 - lam0[layer]] for layer in range(D)], np.float32)
    out["layer_consts"] = np.broadcast_to(rows[:, None, :], (D, P, 3))
    out["consts"], out["onehot"], out["level_masks"] = shape_constants()
    return {k: np.ascontiguousarray(v) for k, v in out.items()}


def program(nc, arrays, known):
    a = {name: nc.dram_tensor(f"in_{name}", v.shape, mybir.dt.from_np(v.dtype), kind="ExternalInput").ap()
         for name, v in arrays.items()}
    a["out"] = nc.dram_tensor("out_0", (P, KT, SEQ), F32, kind="ExternalOutput").ap()
    return layers(nc, a, known)


def kernel(**inputs):
    import concourse.bacc as bacc
    from concourse.bass_utils import run_bass_kernel_spmd

    arrays = lay_out({k: np.asarray(v) for k, v in inputs.items()})
    known = program(bacc.Bacc("TRN2", target_bir_lowering=False, num_devices=1), arrays, {})
    nc = bacc.Bacc("TRN2", target_bir_lowering=False, num_devices=1)
    program(nc, arrays, known)
    r = run_bass_kernel_spmd(nc, [{f"in_{k}": v for k, v in arrays.items()}], core_ids=[0])
    out = r.results[0]["out_0"]
    return out.transpose(1, 0, 2).reshape(D_MODEL, SEQ).T.reshape(1, SEQ, D_MODEL)
```
